# Optimizing a Trainium2 kernel written in Bass

```python
import jax
import jax.numpy as jnp
from jax import lax
import numpy as np

D_MODEL = 1024
BATCH = 1
SEQ = 1024
DEPTH = 2

CHUNK = 64
N_EVEN = (DEPTH + 1) // 2
N_ODD = DEPTH // 2

A_HEADS = 8
A_KV_HEADS = 2
A_HEAD_DIM = 64
A_WINDOW = 128
A_WIN_CHUNKS = A_WINDOW // CHUNK
ROPE_THETA = 10000.0
B_HEADS = 4
B_HEAD_DIM = 128
B_CONV = 4
NORM_EPS = 1e-6
C_WIDTH = D_MODEL
C_HEADS = 4
C_BLOCK = C_WIDTH // C_HEADS
C_CONV = 4
C_EXP = 8.0
N_GROUPS = 4
EXPERTS_PER_GROUP = 8
N_EXPERTS = N_GROUPS * EXPERTS_PER_GROUP
TOP_K_INNER = 2
D_EXPERT = 512
MOE_BLOCK = 128
DN_ALPHA = (2.0 * DEPTH) ** 0.25
DN_BETA = (8.0 * DEPTH) ** -0.25
LN_EPS = 1e-5

A_Q = A_HEADS * A_HEAD_DIM
A_KV = A_KV_HEADS * A_HEAD_DIM
B_W = B_HEADS * B_HEAD_DIM
HYB_IN = A_Q + 2 * A_KV + 4 * B_W + 2 * B_HEADS
HYB_MIX = A_Q + B_W
HYB_SPLITS = [A_Q, A_Q + A_KV, A_Q + 2 * A_KV, A_Q + 2 * A_KV + 3 * B_W,
              A_Q + 2 * A_KV + 4 * B_W, A_Q + 2 * A_KV + 4 * B_W + B_HEADS]

kernel_name = "hybrid_swa_deltanet_rglru_hmoe"

F32 = jnp.float32

def layer_norm(x, g, b):
    xf = x.astype(F32)
    mu = xf.mean(-1, keepdims=True)
    var = jnp.square(xf - mu).mean(-1, keepdims=True)
    return ((xf - mu) * lax.rsqrt(var + LN_EPS) * g.astype(F32) + b.astype(F32)).astype(x.dtype)

def causal_conv(x, w):
    k, c = w.shape
    return lax.conv_general_dilated(x, w[:, None, :].astype(x.dtype), window_strides=(1,),
                                    padding=[(k - 1, 0)], dimension_numbers=('NWC', 'WIO', 'NWC'),
                                    feature_group_count=c)

def rope(x, positions):
    half = x.shape[-1] // 2
    inv = ROPE_THETA ** (-jnp.arange(half, dtype=F32) / half)
    ang = positions.astype(F32)[..., None] * inv
    cos = jnp.cos(ang)[:, :, None, :]
    sin = jnp.sin(ang)[:, :, None, :]
    x1 = x[..., :half].astype(F32)
    x2 = x[..., half:].astype(F32)
    return jnp.concatenate([x1 * cos - x2 * sin, x2 * cos + x1 * sin], -1).astype(x.dtype)

def sliding_window_sink_attention(q, k, v, sinks):
    bn, s_len, h, hd = q.shape
    kv = k.shape[2]
    g = h // kv
    n = s_len // CHUNK
    qc = q.reshape(bn, n, CHUNK, kv, g, hd).astype(F32)

    def band(t):
        tc = t.reshape(bn, n, CHUNK, kv, hd).astype(F32)
        tc = jnp.pad(tc, ((0, 0), (A_WIN_CHUNKS - 1, 0), (0, 0), (0, 0), (0, 0)))
        return jnp.concatenate([tc[:, j:j + n] for j in range(A_WIN_CHUNKS)], axis=2)

    kb = band(k)
    vb = band(v)
    s = jnp.einsum('bnqkgd,bnjkd->bnkgqj', qc, kb) * (hd ** -0.5)
    key_chunk = (jnp.arange(n)[:, None] - (A_WIN_CHUNKS - 1)
                 + (jnp.arange(A_WIN_CHUNKS * CHUNK) // CHUNK)[None, :])
    valid = key_chunk >= 0
    s = jnp.where(valid[None, :, None, None, None, :], s, -jnp.inf)
    sink = sinks.astype(F32).reshape(kv, g)[None, None, :, :, None, None]
    m = jnp.maximum(s.max(-1, keepdims=True), sink)
    p = jnp.exp(s - m)
    denom = p.sum(-1, keepdims=True) + jnp.exp(sink - m)
    o = jnp.einsum('bnkgqj,bnjkd->bnqkgd', p / denom, vb)
    return o.reshape(bn, s_len, h * hd).astype(q.dtype)

def l2norm(x):
    return x * lax.rsqrt(jnp.sum(x * x, -1, keepdims=True) + NORM_EPS)

def gated_delta_rule(q, k, v, g, beta):
    bn, s_len, h, dk = q.shape
    dv = v.shape[-1]
    n = s_len // CHUNK

    def chunks(t):
        return t.reshape(bn, n, CHUNK, h, -1).transpose(0, 1, 3, 2, 4)

    q, k, v = chunks(q), chunks(k), chunks(v)
    g = g.reshape(bn, n, CHUNK, h).transpose(0, 1, 3, 2)
    beta = beta.reshape(bn, n, CHUNK, h).transpose(0, 1, 3, 2)
    g = jnp.cumsum(g, axis=-1)
    tri = jnp.tril(jnp.ones((CHUNK, CHUNK), bool))
    strict = jnp.tril(jnp.ones((CHUNK, CHUNK), bool), -1)
    decay = jnp.exp(jnp.where(tri, g[..., :, None] - g[..., None, :], -jnp.inf))
    k_beta = k * beta[..., None]
    lower = jnp.where(strict, jnp.einsum('bnhid,bnhjd->bnhij', k_beta, k) * decay, 0.0)
    eye = jnp.eye(CHUNK, dtype=F32)
    t_inv = lax.linalg.triangular_solve(eye + lower, jnp.broadcast_to(eye, lower.shape),
                                        left_side=True, lower=True, unit_diagonal=True)
    u = jnp.einsum('bnhij,bnhjd->bnhid', t_inv, v * beta[..., None])
    w = jnp.einsum('bnhij,bnhjd->bnhid', t_inv, k_beta * jnp.exp(g)[..., None])
    attn = jnp.einsum('bnhid,bnhjd->bnhij', q, k) * decay
    q_g = q * jnp.exp(g)[..., None]
    k_g = k * jnp.exp(g[..., -1:] - g)[..., None]
    g_last = jnp.exp(g[..., -1])

    def step(state, xs):
        qg_i, kg_i, u_i, w_i, attn_i, gl_i = xs
        v_new = u_i - jnp.einsum('bhcd,bhde->bhce', w_i, state)
        o = jnp.einsum('bhcd,bhde->bhce', qg_i, state) + jnp.einsum('bhij,bhje->bhie', attn_i, v_new)
        state = state * gl_i[..., None, None] + jnp.einsum('bhcd,bhce->bhde', kg_i, v_new)
        return state, o

    xs = tuple(jnp.moveaxis(t, 1, 0) for t in (q_g, k_g, u, w, attn, g_last))
    state0 = jnp.zeros((bn, h, dk, dv), F32)
    _, o = lax.scan(step, state0, xs)
    return o.transpose(1, 0, 3, 2, 4).reshape(bn, s_len, h, dv)

def hybrid_mixer(x, positions, w_in, sinks, conv_w, a_log, dt_bias, norm_g, w_out):
    bn, s_len, _ = x.shape
    proj = x @ w_in
    aq, ak, av, bqkv, bz, bbeta, ba = jnp.split(proj, HYB_SPLITS, axis=-1)
    q = rope(aq.reshape(bn, s_len, A_HEADS, A_HEAD_DIM), positions)
    k = rope(ak.reshape(bn, s_len, A_KV_HEADS, A_HEAD_DIM), positions)
    v = av.reshape(bn, s_len, A_KV_HEADS, A_HEAD_DIM)
    ya = sliding_window_sink_attention(q, k, v, sinks)
    qkv = jax.nn.silu(causal_conv(bqkv, conv_w).astype(F32))
    bq, bk, bv = jnp.split(qkv, [B_W, 2 * B_W], axis=-1)
    bq = l2norm(bq.reshape(bn, s_len, B_HEADS, B_HEAD_DIM)) * (B_HEAD_DIM ** -0.5)
    bk = l2norm(bk.reshape(bn, s_len, B_HEADS, B_HEAD_DIM))
    bv = bv.reshape(bn, s_len, B_HEADS, B_HEAD_DIM)
    beta = jax.nn.sigmoid(bbeta.astype(F32))
    g = -jnp.exp(a_log.astype(F32)) * jax.nn.softplus(ba.astype(F32) + dt_bias.astype(F32))
    o = gated_delta_rule(bq, bk, bv, g, beta)
    z = bz.reshape(bn, s_len, B_HEADS, B_HEAD_DIM).astype(F32)
    o = o * lax.rsqrt(jnp.mean(o * o, -1, keepdims=True) + NORM_EPS) * norm_g.astype(F32) * jax.nn.silu(z)
    yb = o.reshape(bn, s_len, B_W).astype(x.dtype)
    return jnp.concatenate([ya, yb], axis=-1) @ w_out

def rglru_mixer(x, w_in, conv_w, conv_b, w_a, b_a, w_x, b_x, lam, w_out):
    bn, s_len, _ = x.shape
    proj = x @ w_in
    xg, xr = jnp.split(proj, [C_WIDTH], axis=-1)
    xr = (causal_conv(xr, conv_w) + conv_b).astype(F32)
    xh = xr.reshape(bn, s_len, C_HEADS, C_BLOCK)
    r = jax.nn.sigmoid(jnp.einsum('bshi,hij->bshj', xh, w_a.astype(F32)).reshape(bn, s_len, C_WIDTH) + b_a)
    i = jax.nn.sigmoid(jnp.einsum('bshi,hij->bshj', xh, w_x.astype(F32)).reshape(bn, s_len, C_WIDTH) + b_x)
    log_a = -C_EXP * r * jax.nn.softplus(-lam.astype(F32))
    a = jnp.exp(log_a)
    b = jnp.sqrt(-jnp.expm1(2.0 * log_a)) * (i * xr)

    def combine(left, right):
        al, bl = left
        ar, br = right
        return al * ar, ar * bl + br

    _, h = lax.associative_scan(combine, (a, b), axis=1)
    y = jax.nn.gelu(xg.astype(F32)) * h
    return y.astype(x.dtype) @ w_out

def grouped_expert_ffn(xf, expert_idx, gate, w_gate, w_up, w_down):
    t_len, k_sel = expert_idx.shape
    d = xf.shape[-1]
    n_rows_used = t_len * k_sel
    flat_e = expert_idx.reshape(n_rows_used)
    flat_tok = jnp.arange(n_rows_used, dtype=jnp.int32) // k_sel
    flat_w = gate.reshape(n_rows_used).astype(F32)
    order = jnp.argsort(flat_e)
    se = flat_e[order]
    counts = jnp.bincount(flat_e, length=N_EXPERTS)
    padded = (counts + MOE_BLOCK - 1) // MOE_BLOCK * MOE_BLOCK
    start = jnp.cumsum(counts) - counts
    pad_end = jnp.cumsum(padded)
    pad_start = pad_end - padded
    dest = pad_start[se] + jnp.arange(n_rows_used, dtype=jnp.int32) - start[se]
    n_blocks = n_rows_used // MOE_BLOCK + N_EXPERTS
    n_rows = n_blocks * MOE_BLOCK
    row_tok = jnp.zeros((n_rows,), jnp.int32).at[dest].set(flat_tok[order])
    row_w = jnp.zeros((n_rows,), F32).at[dest].set(flat_w[order])
    block_e = jnp.minimum(jnp.searchsorted(pad_end, jnp.arange(n_blocks) * MOE_BLOCK, side='right'),
                          N_EXPERTS - 1)
    xb = xf[row_tok].reshape(n_blocks, MOE_BLOCK, d)

    def expert_block(args):
        xi, e = args
        hid = jax.nn.silu(xi @ w_gate[e]) * (xi @ w_up[e])
        return hid @ w_down[e]

    yb = lax.map(expert_block, (xb, block_e))
    yw = yb.reshape(n_rows, d).astype(F32) * row_w[:, None]
    return jax.ops.segment_sum(yw, row_tok, num_segments=t_len).astype(xf.dtype)

def hierarchical_moe(x, rg_w, rg_b, re_w, re_b, w_gate, w_up, w_down):
    bn, s_len, d = x.shape
    t_len = bn * s_len
    xf = x.reshape(t_len, d)
    xr = xf.astype(F32)
    tok = jnp.arange(t_len)
    group_logits = xr @ rg_w.astype(F32) + rg_b.astype(F32)
    group_prob = jax.nn.softmax(group_logits, axis=-1)
    g_top = jnp.argmax(group_logits, axis=-1)
    p_top = group_prob[tok, g_top]
    expert_logits = (xr @ re_w.astype(F32) + re_b.astype(F32)).reshape(t_len, N_GROUPS, EXPERTS_PER_GROUP)
    in_group = expert_logits[tok, g_top]
    top_v, top_i = lax.top_k(in_group, TOP_K_INNER)
    expert_idx = g_top[:, None].astype(jnp.int32) * EXPERTS_PER_GROUP + top_i.astype(jnp.int32)
    gate = p_top[:, None] * jax.nn.softmax(top_v, axis=-1)
    y = grouped_expert_ffn(xf, expert_idx, gate, w_gate, w_up, w_down)
    return y.reshape(bn, s_len, d)

def setup_inputs(seed: int = 0) -> dict:
    key = jax.random.key(seed)
    ks = jax.random.split(key, 32)

    def nrm(k, shape, fan_in, scale=1.0):
        return jax.random.normal(k, shape, F32) * (scale * fan_in ** -0.5)

    def small(k, shape, scale=0.01):
        return jax.random.normal(k, shape, F32) * scale

    x = jax.random.normal(ks[0], (BATCH, SEQ, D_MODEL), F32)
    offsets = jax.random.randint(ks[1], (BATCH, 1), 0, 4096, dtype=jnp.int32)
    positions = offsets + jnp.arange(SEQ, dtype=jnp.int32)[None, :]

    dt = jnp.exp(jax.random.uniform(ks[6], (N_EVEN, B_HEADS), F32, np.log(1e-3), np.log(1e-1)))
    u = jax.random.uniform(ks[16], (N_ODD, C_WIDTH), F32, 0.81, 0.998)
    a_base = u ** (1.0 / C_EXP)
    return {
        'x': x,
        'positions': positions,
        'hyb_w_in': nrm(ks[2], (N_EVEN, D_MODEL, HYB_IN), D_MODEL),
        'hyb_sinks': small(ks[3], (N_EVEN, A_HEADS), 0.5),
        'hyb_conv_w': nrm(ks[4], (N_EVEN, B_CONV, 3 * B_W), B_CONV),
        'hyb_a_log': jnp.log(jax.random.uniform(ks[5], (N_EVEN, B_HEADS), F32, 1.0, 16.0)),
        'hyb_dt_bias': dt + jnp.log(-jnp.expm1(-dt)),
        'hyb_norm_g': 1.0 + small(ks[7], (N_EVEN, B_HEAD_DIM), 0.02),
        'hyb_w_out': nrm(ks[8], (N_EVEN, HYB_MIX, D_MODEL), HYB_MIX, DN_BETA),
        'rec_w_in': nrm(ks[9], (N_ODD, D_MODEL, 2 * C_WIDTH), D_MODEL),
        'rec_conv_w': nrm(ks[10], (N_ODD, C_CONV, C_WIDTH), C_CONV),
        'rec_conv_b': small(ks[11], (N_ODD, C_WIDTH)),
        'rec_w_a': nrm(ks[12], (N_ODD, C_HEADS, C_BLOCK, C_BLOCK), C_BLOCK),
        'rec_b_a': small(ks[13], (N_ODD, C_WIDTH)),
        'rec_w_x': nrm(ks[14], (N_ODD, C_HEADS, C_BLOCK, C_BLOCK), C_BLOCK),
        'rec_b_x': small(ks[15], (N_ODD, C_WIDTH)),
        'rec_lambda': jnp.log(a_base) - jnp.log1p(-a_base),
        'rec_w_out': nrm(ks[17], (N_ODD, C_WIDTH, D_MODEL), C_WIDTH, DN_BETA),
        'moe_rg_w': nrm(ks[18], (DEPTH, D_MODEL, N_GROUPS), D_MODEL),
        'moe_rg_b': small(ks[19], (DEPTH, N_GROUPS)),
        'moe_re_w': nrm(ks[20], (DEPTH, D_MODEL, N_EXPERTS), D_MODEL),
        'moe_re_b': small(ks[21], (DEPTH, N_EXPERTS)),
        'moe_w_gate': nrm(ks[22], (DEPTH, N_EXPERTS, D_MODEL, D_EXPERT), D_MODEL),
        'moe_w_up': nrm(ks[23], (DEPTH, N_EXPERTS, D_MODEL, D_EXPERT), D_MODEL),
        'moe_w_down': nrm(ks[24], (DEPTH, N_EXPERTS, D_EXPERT, D_MODEL), D_EXPERT, DN_BETA),
        'ln_g': 1.0 + small(ks[25], (DEPTH, 2, D_MODEL), 0.02),
        'ln_b': small(ks[26], (DEPTH, 2, D_MODEL), 0.02),
    }

def reference(x, positions, hyb_w_in, hyb_sinks, hyb_conv_w, hyb_a_log, hyb_dt_bias, hyb_norm_g,
              hyb_w_out, rec_w_in, rec_conv_w, rec_conv_b, rec_w_a, rec_b_a, rec_w_x, rec_b_x,
              rec_lambda, rec_w_out, moe_rg_w, moe_rg_b, moe_re_w, moe_re_b, moe_w_gate, moe_w_up,
              moe_w_down, ln_g, ln_b):
    h = x
    for layer in range(DEPTH):
        i = layer // 2
        if layer % 2 == 0:
            mix = hybrid_mixer(h, positions, hyb_w_in[i], hyb_sinks[i], hyb_conv_w[i], hyb_a_log[i],
                               hyb_dt_bias[i], hyb_norm_g[i], hyb_w_out[i])
        else:
            mix = rglru_mixer(h, rec_w_in[i], rec_conv_w[i], rec_conv_b[i], rec_w_a[i], rec_b_a[i],
                              rec_w_x[i], rec_b_x[i], rec_lambda[i], rec_w_out[i])
        h = layer_norm(DN_ALPHA * h + mix, ln_g[layer, 0], ln_b[layer, 0])
        ffn = hierarchical_moe(h, moe_rg_w[layer], moe_rg_b[layer], moe_re_w[layer], moe_re_b[layer],
                               moe_w_gate[layer], moe_w_up[layer], moe_w_down[layer])
        h = layer_norm(DN_ALPHA * h + ffn, ln_g[layer, 1], ln_b[layer, 1])
    return h


_drawn_inputs = setup_inputs


def setup_inputs(seed=0):
    import zlib

    import numpy as np

    out = dict(_drawn_inputs(seed))
    spreads = {}
    factors = {'hyb_sinks': 31.003,
     'hyb_a_log': 3.641,
     'hyb_norm_g': 22.929,
     'rec_conv_b': 4.502,
     'rec_b_a': 64.0,
     'rec_b_x': 64.0,
     'moe_rg_b': 20.812,
     'moe_re_b': 21.608}
    for name, (base, spread) in spreads.items():
        noise = np.random.default_rng([zlib.crc32(name.encode()), seed]).standard_normal(out[name].shape)
        drawn = base * np.exp(spread * noise) if base else spread * noise
        out[name] = jnp.asarray(drawn.astype(out[name].dtype))
    for name, factor in factors.items():
        out[name] = (out[name] * factor).astype(out[name].dtype)
    return out
```

```python
from contextlib import ExitStack

import numpy as np

import concourse.bass as bass
from concourse import mybir
from concourse.alu_op_type import AluOpType as ALU

ACT = mybir.ActivationFunctionType
F32 = mybir.dt.float32
I32 = mybir.dt.int32
AX = mybir.AxisListType.X

P = 128
SEQ = 1024
D = 1024
NT = SEQ // P
KC = D // P
HALF = 512

A_HEADS, A_KV, A_HD = 8, 2, 64
B_HEADS = 4
CONV = 4
WIN = 2 * P
THETA = 10000.0
NORM_EPS, LN_EPS = 1e-6, 1e-5
ALPHA = 4.0 ** 0.25

GROUPS, PER_GROUP = 4, 8
EXPERTS = GROUPS * PER_GROUP
ROUTES = GROUPS + EXPERTS
F = 512
FC = F // P
OVERFLOW = 16
BLOCKS = EXPERTS + OVERFLOW
TABLE = BLOCKS + 2
NOBODY = 1 << 20

LEVELS = 7
N_CH = 17
N_QK = 5

C_ID, C_UTRI, C_USTRICT, C_ONES = 0, P, 2 * P, 3 * P
C_LEVEL = 4 * P
C_AMASK = C_LEVEL + LEVELS * P
C_PERM = C_AMASK + WIN
C_IOTA = C_PERM + P
C_INV = C_IOTA + P
C_TOKEN = C_INV + 1
C_STEP = C_TOKEN + NT
N_CONST = C_STEP + 8

R_SINK, R_ALOG, R_DT, R_NORM = 0, 8, 12, 16
R_ROUTE = 16 + P
N_ROW = R_ROUTE + 2 * ROUTES


def constants():
    c = np.zeros((P, N_CONST), np.float32)
    p = np.arange(P)
    i, j = p[:, None], p[None, :]
    c[:, C_ID:C_ID + P] = i == j
    c[:, C_UTRI:C_UTRI + P] = i <= j
    c[:, C_USTRICT:C_USTRICT + P] = i < j
    c[:, C_ONES:C_ONES + P] = 1.0
    for level in range(LEVELS):
        s = 1 << level
        m = (i // (2 * s) == j // (2 * s)) & ((j // s) % 2 == 1) & ((i // s) % 2 == 0)
        c[:, C_LEVEL + level * P:C_LEVEL + (level + 1) * P] = m
    key = np.arange(WIN)[None, :]
    first = (i < P // 2) & (key >= P // 2) & (key < 3 * P // 2)
    second = (i >= P // 2) & (key >= P)
    c[:, C_AMASK:C_AMASK + WIN] = np.where(first | second, 0.0, -1e30)
    half = A_HD // 2
    for d in range(P):
        if d % A_HD < half:
            c[d + half, C_PERM + d] = -1.0
        else:
            c[d - half, C_PERM + d] = 1.0
    c[:, C_IOTA:C_IOTA + P] = j
    inv = np.float32(THETA) ** (-np.arange(half, dtype=np.float32) / np.float32(half))
    c[:, C_INV] = inv[p % half]
    for t in range(NT):
        c[:, C_TOKEN + t] = t * P + p + 1
    c[:, C_STEP:C_STEP + 8] = 2 * np.arange(8)
    return c


class Steps:

    def __init__(self, eng, sem, base=0):
        self.eng, self.sem, self.base, self.n = eng, sem, base, 0

    def link(self, ins):
        self.n += 1
        ins.then_inc(self.sem, 1)
        self.eng.wait_ge(self.sem, self.base + self.n)


def program(nc, a, out, stop=None):
    ctx = ExitStack()
    with ctx:
        def sb(name, shape, dt=F32, scope=ctx):
            return scope.enter_context(nc.sbuf_tensor(name, shape, dt))

        stage_sems = []

        def sem(name):
            stage_sems.append(nc.alloc_semaphore(name))
            return stage_sems[-1]

        def end_stage():
            nc.clear_and_free_semaphores(list(stage_sems))
            nc.all_engine_barrier()
            stage_sems.clear()

        h_dram = nc.dram_tensor("h_rows", (SEQ, D), F32, kind="Internal").ap()
        y_dram = nc.dram_tensor("expert_rows", (2 * SEQ, D), F32, kind="Internal").ap()

        ps = ctx.enter_context(nc.psum_tensor("ps", [P, 8, HALF], F32))
        h = sb("h", [P, NT, D])
        hT = sb("hT", [P, KC, SEQ])
        cst = sb("cst", [P, N_CONST])
        rows = sb("rows", [P, N_ROW])
        gates = sb("gates", [P, 2, NT])
        src_idx = sb("src_idx", [P, TABLE], I32)
        dst_idx = sb("dst_idx", [P, TABLE], I32)
        ctl = sb("ctl", [1, TABLE + 1], I32)

        m = Machine(nc, a, sb, sem, ps, h, hT, cst, rows, gates, src_idx, dst_idx, ctl, h_dram, y_dram)
        hybrid(m)
        end_stage()
        for layer in range(2):
            if layer == 1:
                recurrent(m)
            experts = ExitStack()
            with experts:
                wgu = sb(f"wgu{layer}", [P, 2, 2, KC, F], scope=experts)
                wd = sb(f"wd{layer}", [P, 2, FC, D], scope=experts)
                w_sems = [[sem(f"{kind}_loaded{layer}{j}") for j in range(2)] for kind in ("gate", "up", "down")]
                out_projection(m, layer, wgu, wd, w_sems)
                if stop == f"ln{layer}":
                    return finish(m, out)
                router(m, layer, wd, w_sems)
                expert_blocks(m, layer, wgu, wd, w_sems)
            combine(m, layer, out if layer == 1 else None)
            if stop == f"moe{layer}":
                return finish(m, out)
            end_stage()


def finish(m, out):
    done = m.sem("dbg")
    with m.nc.Block() as block:
        @block.sync
        def _(sp):
            sp.dma_start(out[0].rearrange("(t p) d -> p t d", p=P), m.h[:]).then_inc(done, 16)
            sp.wait_ge(done, 16)


class Machine:

    def __init__(self, nc, a, sb, sem, ps, h, hT, cst, rows, gates, src_idx, dst_idx, ctl, h_dram, y_dram):
        self.nc, self.a, self.sb, self.sem = nc, a, sb, sem
        self.ps, self.h, self.hT, self.cst, self.rows = ps, h, hT, cst, rows
        self.gates, self.src_idx, self.dst_idx, self.ctl = gates, src_idx, dst_idx, ctl
        self.h_dram, self.y_dram = h_dram, y_dram
        self.scratch = nc.dram_tensor("scratch", (2, P, 2), I32, kind="Internal").ap()

    def c(self, at, n=P):
        return self.cst[:, at:at + n]


def log1p_steps(v, steps, out, e, z, z2, poly):
    terms = 8
    steps.link(v.tensor_scalar(z, e, 2.0, None, ALU.add))
    steps.link(v.reciprocal(z, z))
    steps.link(v.tensor_tensor(z, e, z, ALU.mult))
    steps.link(v.tensor_tensor(z2, z, z, ALU.mult))
    steps.link(v.tensor_scalar(poly, z2, 1.0 / (2 * terms + 1), 1.0 / (2 * terms - 1), ALU.mult, ALU.add))
    for n in range(terms - 2, -1, -1):
        steps.link(v.tensor_tensor(poly, poly, z2, ALU.mult))
        steps.link(v.tensor_scalar(poly, poly, 1.0 / (2 * n + 1), None, ALU.add))
    steps.link(v.scalar_tensor_tensor(out, z, 2.0, poly, ALU.mult, ALU.mult))


def hybrid(m):
    nc, a, sb, sem = m.nc, m.a, m.sb, m.sem
    scope = ExitStack()
    with scope:
        z = sb("z", [P, NT, HALF], scope=scope)
        bkq = sb("bkq", [P, 2, B_HEADS, SEQ], scope=scope)
        vb = sb("vb", [P, NT, B_HEADS, P], scope=scope)
        beta = sb("beta", [P, NT, B_HEADS], scope=scope)
        g_raw = sb("g_raw", [P, NT, B_HEADS], scope=scope)
        inner = ExitStack()
        with inner:
            qT = sb("qT", [P, 4, SEQ], scope=inner)
            kT = sb("kT", [P, SEQ], scope=inner)
            v_tok = sb("v_tok", [P, NT, P], scope=inner)
            project(m, qT, kT, v_tok, z, bkq, vb, beta, g_raw)
            attention(m, qT, kT, v_tok)
        delta_net(m, z, bkq, vb, beta, g_raw)


def project(m, qT, kT, v_tok, z, bkq, vb, beta, g_raw):
    nc, a, sb, sem, ps, hT = m.nc, m.a, m.sb, m.sem, m.ps, m.hT
    scope = ExitStack()
    with scope:
        w_vs = sb("w_vs", [P, KC, P + 8], scope=scope)
        w_z = sb("w_z", [P, KC, HALF], scope=scope)
        w_ch = sb("w_ch", [P, 2, KC, P], scope=scope)
        conv_w = sb("conv_w", [P, 12, CONV], scope=scope)
        cos, sin, pos = m.h[:, 0, :], m.h[:, 1, :], m.h[:, 2, :].bitcast(I32)
        raw = sb("raw", [P, 2, CONV - 1 + SEQ], scope=scope)
        small = sb("small", [P, NT, 8], scope=scope)
        eps = sb("eps", [P, 1], scope=scope)
        soft = sb("soft", [P, 6, NT * B_HEADS], scope=scope)
        acc = w_z[:, 0:2, :].rearrange("p a b -> p (a b)")
        sq = w_z[:, 2:6, :].rearrange("p (s a) b -> p s (a b)", s=2)
        tmp = w_z[:, 6:8, :].rearrange("p a b -> p (a b)")

        s_in, s_x, s_wv, s_wz = sem("const_in"), sem("x_in"), sem("wv_in"), sem("wz_in")
        s_w = [sem(f"w_ch_in{j}") for j in range(2)]
        proj, evac, post, fin = sem("projected"), sem("evacuated"), sem("posted"), sem("finished")
        conv, silu = sem("convolved"), sem("activated")
        s_dve, s_act, rooted = sem("proj_dve"), sem("proj_act"), sem("proj_rooted")
        ang, trig, soft_in, soft_out, zero = sem("angle"), sem("trig"), sem("soft_in"), sem("soft_out"), sem("padded")
        PI = float(np.float32(3.1415925))

        with nc.Block() as block:
            @block.sync
            def _(sp):
                sp.dma_start(m.cst[:], a["cst"]).then_inc(s_in, 16)
                sp.dma_start(m.rows[:], a["rows"].partition_broadcast(P)).then_inc(s_in, 16)
                sp.dma_start(pos, a["positions"].partition_broadcast(P)).then_inc(s_in, 16)
                sp.dma_start(conv_w[:], a["conv_w"]).then_inc(s_in, 16)
                sp.dma_start(w_vs[:], a["w_vs"]).then_inc(s_wv, 16)
                for q in range(4):
                    sp.dma_start(hT[:, 2 * q:2 * q + 2, :], a["xT"][:, 2 * q:2 * q + 2, :]).then_inc(s_x, 16)
                sp.dma_start(w_z[:], a["w_z"]).then_inc(s_wz, 16)
                for n in range(N_CH):
                    if n >= 2:
                        sp.wait_ge(proj, 2 * NT + n - 1)
                    sp.dma_start(w_ch[:, n % 2], a["w_ch"][n]).then_inc(s_w[n % 2], 16)

            @block.tensor
            def _(pe):
                pe.wait_ge(s_wv, 16)
                pe.wait_ge(s_x, 64)
                for g in range(2 * NT):
                    t = g % NT
                    w, n = (w_vs, P + 8) if g < NT else (w_z, HALF)
                    if g == NT:
                        pe.wait_ge(s_wz, 16)
                    if g >= 4:
                        pe.wait_ge(evac, g - 3)
                    for c in range(KC):
                        mm = pe.matmul(ps[:, g % 4, 0:n], hT[:, c, t * P:(t + 1) * P], w[:, c, :],
                                       start=(c == 0), stop=(c == KC - 1))
                    mm.then_inc(proj, 1)

                def main(n):
                    pe.wait_ge(s_w[n % 2], 16 * (n // 2 + 1))
                    pe.wait_ge(evac, 2 * NT if n < 2 else 2 * NT + n - 1)
                    for u in range(2):
                        for c in range(KC):
                            mm = pe.matmul(ps[:, 2 * (n % 2) + u, :], w_ch[:, n % 2, c, :],
                                           hT[:, c, u * HALF:(u + 1) * HALF], start=(c == 0), stop=(c == KC - 1))
                    mm.then_inc(proj, 1)

                def after(n):
                    if n == 0:
                        pe.wait_ge(s_in, 64)
                    if n < N_QK:
                        pe.wait_ge(evac, 2 * NT + n + 1)
                    else:
                        pe.wait_ge(silu, n - N_QK + 1)
                    if n >= 2:
                        pe.wait_ge(fin, n - 1)
                    b = 4 + 2 * (n % 2)
                    if n < 13:
                        lhs = m.c(C_PERM) if n < N_QK else m.c(C_ONES)
                        for u in range(2):
                            rhs = (raw[:, n % 2, CONV - 1 + u * HALF:CONV - 1 + (u + 1) * HALF] if n < N_QK
                                   else sq[:, n % 2, u * HALF:(u + 1) * HALF])
                            mm = pe.matmul(ps[:, b + u, :], lhs, rhs, start=True, stop=True)
                    else:
                        for t in range(NT):
                            mm = pe.transpose(ps[:, b + t // 4, (t % 4) * P:(t % 4 + 1) * P],
                                              sq[:, n % 2, t * P:(t + 1) * P], m.c(C_ID))
                    mm.then_inc(post, 1)

                for n in range(N_CH):
                    main(n)
                    if n:
                        after(n - 1)
                after(N_CH - 1)

            @block.scalar
            def _(act):
                steps = Steps(act, s_act)
                for g in range(2 * NT):
                    t = g % NT
                    act.wait_ge(proj, g + 1)
                    if g < NT:
                        steps.link(act.activation(v_tok[:, t, :], ps[:, g % 4, 0:P], ACT.Copy))
                        act.activation(small[:, t, :], ps[:, g % 4, P:P + 8], ACT.Copy).then_inc(evac, 1)
                    else:
                        act.activation(z[:, t, :], ps[:, g % 4, :], ACT.Silu).then_inc(evac, 1)
                act.wait_ge(ang, 1)
                act.activation(sin, sin, ACT.Sin).then_inc(trig, 1)
                act.activation(cos, cos, ACT.Sin).then_inc(trig, 1)
                act.wait_ge(evac, NT)
                act.activation(beta[:], small[:, :, 0:4], ACT.Sigmoid).then_inc(soft_out, 1)
                act.wait_ge(soft_in, 1)
                act.activation(soft[:, 1, :], soft[:, 1, :], ACT.Exp, scale=-1.0).then_inc(soft_out, 1)
                act.wait_ge(s_in, 64)
                act.activation(soft[:, 5, 0:4], m.rows[:, R_ALOG:R_ALOG + 4], ACT.Exp).then_inc(soft_out, 1)
                act.wait_ge(zero, 1)

                def root(n):
                    act.wait_ge(post, n + 1)
                    act.wait_ge(fin, n)
                    act.activation(tmp.rearrange("p (u f) -> p u f", u=2), ps[:, 4 + 2 * (n % 2):6 + 2 * (n % 2), :],
                                   ACT.Sqrt, bias=eps[:, 0:1]).then_inc(rooted, 1)

                for n in range(N_CH):
                    act.wait_ge(proj, 2 * NT + n + 1)
                    if n >= 2:
                        act.wait_ge(fin, n - 1)
                    act.activation(raw[:, n % 2, CONV - 1:].rearrange("p (u f) -> p u f", u=2),
                                   ps[:, 2 * (n % 2):2 * (n % 2) + 2, :], ACT.Copy).then_inc(evac, 1)
                    if n >= N_QK:
                        act.wait_ge(conv, n - N_QK + 1)
                        if n < 13:
                            kq, i = (1, n - N_QK) if n < 9 else (0, n - 9)
                            steps.link(act.activation(bkq[:, kq, i, :], acc, ACT.Silu))
                            act.activation(sq[:, n % 2, :], bkq[:, kq, i, :], ACT.Square).then_inc(silu, 1)
                        else:
                            act.activation(sq[:, n % 2, :], acc, ACT.Silu).then_inc(silu, 1)
                    if N_QK <= n - 1 < 13:
                        root(n - 1)

            @block.vector
            def _(v):
                steps = Steps(v, s_dve)
                steps.link(v.memset(eps[:], NORM_EPS))
                v.memset(raw[:, :, 0:CONV - 1], 0.0).then_inc(zero, 1)
                v.wait_ge(s_in, 64)
                turns, angle = raw[:, 0, CONV - 1:], raw[:, 1, CONV - 1:]
                steps.link(v.tensor_copy(sin, pos))
                steps.link(v.tensor_scalar(angle, sin, m.c(C_INV, 1), None, ALU.mult))
                two_pi = 2.0 * np.pi
                p1 = 6.28125
                p2 = float(np.float32(np.round((two_pi - p1) * 2 ** 20) / 2 ** 20))
                p3 = float(np.float32(two_pi - p1 - p2))
                magic = float(1.5 * 2 ** 23)
                for k, dst in enumerate((sin, cos)):
                    steps.link(v.tensor_scalar(turns, angle, float(np.float32(1.0 / two_pi)), 0.25 * k, ALU.mult, ALU.add))
                    steps.link(v.tensor_scalar(turns, turns, magic, None, ALU.add))
                    steps.link(v.tensor_scalar(turns, turns, magic, None, ALU.subtract))
                    steps.link(v.scalar_tensor_tensor(dst, turns, -p1, angle, ALU.mult, ALU.add))
                    steps.link(v.scalar_tensor_tensor(dst, turns, -p2, dst, ALU.mult, ALU.add))
                    steps.link(v.scalar_tensor_tensor(dst, turns, -p3, dst, ALU.mult, ALU.add))
                    if k:
                        steps.link(v.tensor_scalar(dst, dst, float(np.pi / 2), None, ALU.add))
                    last = v.tensor_scalar(dst, dst, PI, -PI, ALU.min, ALU.max)
                    if k:
                        last.then_inc(ang, 1)
                    else:
                        steps.link(last)
                v.wait_ge(evac, NT)
                x = soft[:, 0, :]
                dt_row = m.rows[:, None, R_DT:R_DT + 4].to_broadcast([P, NT, 4])
                steps.link(v.tensor_tensor(x.rearrange("p (t f) -> p t f", f=4), small[:, :, 4:8], dt_row, ALU.add))
                steps.link(v.tensor_scalar(soft[:, 2, :], x, -1.0, None, ALU.mult))
                v.tensor_tensor(soft[:, 1, :], x, soft[:, 2, :], ALU.max).then_inc(soft_in, 1)
                v.wait_ge(soft_out, 3)
                log1p_steps(v, steps, soft[:, 1, :], soft[:, 1, :], soft[:, 2, :], soft[:, 3, :], soft[:, 4, :])
                steps.link(v.scalar_tensor_tensor(x, x, 0.0, soft[:, 1, :], ALU.max, ALU.add))
                rate = soft[:, 5:6, 0:4].to_broadcast([P, NT, 4])
                steps.link(v.tensor_tensor(g_raw[:], x.rearrange("p (t f) -> p t f", f=4), rate, ALU.mult))
                steps.link(v.tensor_scalar(g_raw[:], g_raw[:], -1.0, None, ALU.mult))
                v.wait_ge(evac, 2 * NT)
                v.wait_ge(trig, 2)

                def finish_tile(n):
                    v.wait_ge(post, n + 1)
                    both = ps[:, 4 + 2 * (n % 2):6 + 2 * (n % 2), :]
                    halves = lambda x: x.rearrange("p (u f) -> p u f", u=2)
                    if n < N_QK:
                        dst = qT[:, n, :] if n < 4 else kT[:]
                        steps.link(v.tensor_tensor(dst, raw[:, n % 2, CONV - 1:], cos, ALU.mult))
                        steps.link(v.tensor_tensor(halves(tmp), both, halves(sin), ALU.mult))
                        v.tensor_tensor(dst, dst, tmp, ALU.add).then_inc(fin, 1)
                    elif n < 13:
                        kq, i = (1, n - N_QK) if n < 9 else (0, n - 9)
                        v.wait_ge(rooted, n - N_QK + 1)
                        steps.link(v.reciprocal(tmp, tmp))
                        v.scalar_tensor_tensor(bkq[:, kq, i, :], tmp, P ** -0.5 if kq else 1.0, bkq[:, kq, i, :],
                                               ALU.mult, ALU.mult).then_inc(fin, 1)
                    else:
                        i = n - 13
                        v.tensor_tensor(vb[:, :, i, :], both.rearrange("p u (t f) -> p (u t) f", f=P),
                                        beta[:, :, i:i + 1].to_broadcast([P, NT, P]), ALU.mult).then_inc(fin, 1)

                for n in range(N_CH):
                    if n >= N_QK:
                        i = n - N_QK
                        v.wait_ge(evac, 2 * NT + n + 1)
                        if i:
                            v.wait_ge(silu, i)
                        steps.link(v.tensor_scalar(acc, raw[:, n % 2, 0:SEQ], conv_w[:, i, 0:1], None, ALU.mult))
                        for k in range(1, CONV):
                            ins = v.scalar_tensor_tensor(acc, raw[:, n % 2, k:k + SEQ], conv_w[:, i, k:k + 1], acc,
                                                         ALU.mult, ALU.add)
                            if k < CONV - 1:
                                steps.link(ins)
                        ins.then_inc(conv, 1)
                    if n:
                        finish_tile(n - 1)
                finish_tile(N_CH - 1)


def attention(m, qT, kT, v_tok):
    nc, sb, sem, ps, hT = m.nc, m.sb, m.sem, m.ps, m.hT
    scope = ExitStack()
    with scope:
        s = sb("scores", [P, 2, A_HEADS, WIN], scope=scope)
        pT = sb("pT", [P, A_HEADS, 2, P], scope=scope)
        ya = sb("ya", [P, 2, HALF], scope=scope)
        mx = sb("mx", [P, 2, 4, A_HEADS], scope=scope)
        scored, masked, expd = sem("scored"), sem("masked"), sem("exponentiated")
        turned, p_out, mixed, y_out, y_turned, y_done = (sem(x) for x in
            ("p_turned", "p_out", "pv_done", "ya_out", "ya_turned", "ya_done"))
        s_dve, s_sum = sem("att_dve"), sem("denominators")
        maxed, expsink = sem("maxed"), sem("expsink")
        s_h = sem("h_in")

        with nc.Block() as block:
            @block.sync
            def _(sp):
                sp.dma_start(m.h[:], m.a["x"].rearrange("(t p) d -> p t d", p=P)).then_inc(s_h, 16)
                sp.wait_ge(s_h, 16)

            @block.tensor
            def _(pe):
                def scores(t):
                    if t:
                        pe.wait_ge(masked, t)
                    lo = 0 if t else P
                    for hd in range(A_HEADS):
                        b, i = 64 * (hd // 4), hd % 4
                        mm = pe.matmul(ps[:, hd // 2, (hd % 2) * WIN + lo:(hd % 2 + 1) * WIN],
                                       qT[b:b + 64, i, t * P:(t + 1) * P],
                                       kT[b:b + 64, (t - 1) * P + lo:(t + 1) * P], start=True, stop=True)
                    mm.then_inc(scored, 1)

                def values(t):
                    pe.wait_ge(expd, t + 1)
                    for q in range(2):
                        if 2 * t + q:
                            pe.wait_ge(p_out, 2 * t + q)
                        for hd in range(4 * q, 4 * q + 4):
                            for k in range(0 if t else 1, 2):
                                at = (hd - 4 * q) * 2 + k
                                mm = pe.transpose(ps[:, 4 + at // 4, (at % 4) * P:(at % 4 + 1) * P],
                                                  s[:, t % 2, hd, k * P:(k + 1) * P], m.c(C_ID))
                        mm.then_inc(turned, 1)
                    pe.wait_ge(p_out, 2 * t + 2)
                    if t:
                        pe.wait_ge(y_out, t)
                    for hd in range(A_HEADS):
                        b = 64 * (hd // 4)
                        for k in range(0 if t else 1, 2):
                            mm = pe.matmul(ps[:, 6, hd * 64:(hd + 1) * 64], pT[:, hd, k, :],
                                           v_tok[:, t - 1 + k, b:b + 64], start=(k == (0 if t else 1)), stop=(k == 1))
                    mm.then_inc(mixed, 1)

                def turn_y(t):
                    pe.wait_ge(y_out, t + 1)
                    if t:
                        pe.wait_ge(y_done, t)
                    for c in range(4):
                        mm = pe.transpose(ps[:, 7, c * P:(c + 1) * P], ya[:, t % 2, c * P:(c + 1) * P], m.c(C_ID))
                    mm.then_inc(y_turned, 1)

                for t in range(NT + 2):
                    if t < NT:
                        scores(t)
                    if 1 <= t <= NT:
                        values(t - 1)
                    if t >= 2:
                        turn_y(t - 2)

            @block.vector
            def _(v):
                steps = Steps(v, s_dve)

                def softmax_in(t):
                    v.wait_ge(scored, t + 1)
                    if t >= 2:
                        v.wait_ge(turned, 2 * t - 2)
                    lo = 0 if t else P
                    n = WIN - lo
                    sc = s[:, t % 2, :, lo:]
                    raw = ps[:, 0:4, :].rearrange("p b (h w) -> p (b h) w", w=WIN)[:, :, lo:]
                    mask = m.cst[:, None, C_AMASK + lo:C_AMASK + WIN].to_broadcast([P, A_HEADS, n])
                    ins = v.scalar_tensor_tensor(sc, raw, A_HD ** -0.5, mask, ALU.mult, ALU.add)
                    ins.then_inc(masked, 1)
                    v.wait_ge(masked, t + 1)
                    mt = mx[:, t % 2]
                    steps.link(v.tensor_reduce(mt[:, 0, :], sc, AX, ALU.max))
                    steps.link(v.tensor_tensor(mt[:, 0, :], mt[:, 0, :], m.rows[:, R_SINK:R_SINK + 8], ALU.max))
                    steps.link(v.tensor_tensor(mt[:, 1, :], m.rows[:, R_SINK:R_SINK + 8], mt[:, 0, :], ALU.subtract))
                    v.tensor_scalar(mt[:, 0, :], mt[:, 0, :], -1.0, None, ALU.mult).then_inc(maxed, 1)

                def normalise(t):
                    mt = mx[:, t % 2]
                    v.wait_ge(expd, t + 1)
                    steps.link(v.tensor_tensor(mt[:, 2, :], mt[:, 2, :], mt[:, 1, :], ALU.add))
                    steps.link(v.reciprocal(mt[:, 3, :], mt[:, 2, :]))
                    v.wait_ge(mixed, t + 1)
                    if t >= 2:
                        v.wait_ge(y_turned, t - 1)
                    v.tensor_tensor(ya[:, t % 2, :].rearrange("p (h d) -> p h d", d=64),
                                    ps[:, 6, :].rearrange("p (h d) -> p h d", d=64),
                                    mt[:, 3, :, None].to_broadcast([P, A_HEADS, 64]), ALU.mult).then_inc(y_out, 1)

                for t in range(NT + 1):
                    if t < NT:
                        softmax_in(t)
                    if t:
                        normalise(t - 1)

            @block.scalar
            def _(act):
                def exps(t):
                    act.wait_ge(maxed, t + 1)
                    lo = 0 if t else P
                    mt = mx[:, t % 2]
                    act.activation(mt[:, 1, :], mt[:, 1, :], ACT.Exp).then_inc(expsink, 1)
                    for hd in range(A_HEADS):
                        ins = act.activation(s[:, t % 2, hd, lo:], s[:, t % 2, hd, lo:], ACT.Exp,
                                             bias=mt[:, 0, hd:hd + 1], accum_out=mt[:, 2, hd:hd + 1])
                    act.wait_ge(expsink, t + 1)
                    ins.then_inc(expd, 1)

                def copies(t):
                    for q in range(2):
                        act.wait_ge(turned, 2 * t + q + 1)
                        if q == 0 and t:
                            act.wait_ge(mixed, t)
                        lo = 0 if t else 1
                        act.activation(pT[:, 4 * q:4 * q + 4, lo:, :],
                                       ps[:, 4:6, :].rearrange("p b (h k w) -> p (b h) k w", k=2, w=P)[:, :, lo:, :],
                                       ACT.Copy).then_inc(p_out, 1)

                def y_copy(t):
                    act.wait_ge(y_turned, t + 1)
                    act.activation(hT[:, 0:4, t * P:(t + 1) * P], ps[:, 7, :].rearrange("p (c w) -> p c w", w=P),
                                   ACT.Copy).then_inc(y_done, 1)

                for t in range(NT + 2):
                    if t < NT:
                        exps(t)
                    if 1 <= t <= NT:
                        copies(t - 1)
                    if t >= 2:
                        y_copy(t - 2)


def delta_net(m, z, bkq, vb, beta, g_raw):
    nc, sb, sem, ps, hT = m.nc, m.sb, m.sem, m.ps, m.hT
    scope = ExitStack()
    H, L = B_HEADS, LEVELS
    with scope:
        def tile(name, k=2):
            return sb(name, [P, k, H, P], scope=scope)

        diag, decay, expg = tile("diag"), tile("decay"), tile("expg")
        AT, attnT, kbg, kg, qg = tile("AT"), tile("attnT"), tile("kbg"), tile("kg"), tile("qg")
        CT, X, T, TT = tile("CT"), tile("X"), tile("T"), tile("TT")
        state = tile("state", 1)[:, 0]
        wT, u, v_new, o = CT, X, T, AT
        junk = diag
        Gc = sb("Gc", [P, NT, H], scope=scope)
        bg = sb("bg", [P, NT, H], scope=scope)
        kgs = sb("kgs", [P, 2, H], scope=scope)
        ms = sb("ms", [P, 2, H], scope=scope)
        eps = sb("dn_eps", [P, 1], scope=scope)

        bank = lambda b: ps[:, b, :].rearrange("p (h w) -> p h w", w=P)
        col = lambda x: x[:, :, None].to_broadcast([P, H, P])
        mat = lambda at: m.cst[:, None, at:at + P].to_broadcast([P, H, P])
        span = lambda t: slice(t * P, (t + 1) * P)

        summed, gc_out, bg_exp, s_dve, s_act = (sem(f"dn_{x}") for x in ("summed", "gc", "bg_exp", "dve", "act"))
        diagd, gb, diff, expd, masked, qg_out = (sem(f"dn_{x}") for x in ("diag", "gb", "diff", "exp", "mask", "qg"))
        kk, k_turned, at_out, keys_out = (sem(f"dn_{x}") for x in ("kk", "k_turned", "at", "keys"))
        ct_out, x_mm, x_out, tx_mm, t_out = (sem(f"dn_{x}") for x in ("ct", "x_mm", "x_out", "tx_mm", "t_out"))
        uw_mm, uw_out, p1_mm, v_out, o_mm, s_out = (sem(f"dn_{x}") for x in
            ("uw_mm", "uw_out", "p1", "v_new", "o_mm", "state"))
        squared, rms_out = sem("dn_squared"), sem("dn_rms")
        y_out, y_turned, y_done = (sem(f"dn_{x}") for x in ("y", "y_turned", "y_done"))

        lv = lambda t, l: (t // 2) * 2 * L + 2 * l + t % 2 + 1

        with nc.Block() as block:
            @block.tensor
            def _(pe):
                pe.matmul(ps[:, 0, 0:NT * H], m.c(C_UTRI), g_raw[:].rearrange("p t h -> p (t h)"),
                          start=True, stop=True).then_inc(summed, 1)
                for pair in range(NT // 2):
                    ts = (2 * pair, 2 * pair + 1)
                    for t in ts:
                        j = t % 2
                        pe.wait_ge(diagd, t + 1)
                        if t >= 2:
                            pe.wait_ge(y_done, t - 1)
                        pe.matmul(ps[:, 4 * j, :], m.c(C_ONES), diag[:, j].rearrange("p h w -> p (h w)"),
                                  start=True, stop=True).then_inc(gb, 1)
                    for t in ts:
                        j = t % 2
                        if t >= 2:
                            pe.wait_ge(y_out, t - 1)
                            pe.wait_ge(s_out, t)
                        for hd in range(H):
                            mm = pe.matmul(ps[:, 4 * j + 1 + hd // 2, (hd % 2) * 2 * P:(hd % 2 + 1) * 2 * P]
                                           .rearrange("p (a w) -> p a w", a=2),
                                           bkq[:, 0, hd, span(t)], bkq[:, :, hd, span(t)], start=True, stop=True)
                        mm.then_inc(kk, 1)
                        for hd in range(H):
                            mm = pe.transpose(ps[:, 4 * j + 3, hd * P:(hd + 1) * P], bkq[:, 0, hd, span(t)], m.c(C_ID))
                        mm.then_inc(k_turned, 1)
                    for l in range(L):
                        for t in ts:
                            j = t % 2
                            pe.wait_ge(ct_out, lv(t, l))
                            if l:
                                pe.wait_ge(t_out, lv(t, l - 1))
                            else:
                                pe.wait_ge(expd, t + 1)
                            for hd in range(H):
                                o_ = ps[:, 4 * j, hd * P:(hd + 1) * P]
                                if l:
                                    mm = pe.matmul(o_, CT[:, j, hd], T[:, j, hd], start=True, stop=True)
                                else:
                                    mm = pe.transpose(o_, CT[:, j, hd], m.c(C_ID))
                            mm.then_inc(x_mm, 1)
                        for t in ts:
                            j = t % 2
                            pe.wait_ge(x_out, lv(t, l))
                            for hd in range(H):
                                w = slice(hd * P, (hd + 1) * P)
                                if l == 0:
                                    mm = pe.transpose(ps[:, 4 * j + 2, w], X[:, j, hd], m.c(C_ID))
                                else:
                                    if l < L - 1:
                                        pe.matmul(ps[:, 4 * j + 1, w], TT[:, j, hd], X[:, j, hd], start=True, stop=True)
                                    mm = pe.matmul(ps[:, 4 * j + 2, w], X[:, j, hd], TT[:, j, hd], start=True, stop=True)
                            mm.then_inc(tx_mm, 1)
                    for t in ts:
                        j = t % 2
                        pe.wait_ge(t_out, lv(t, L - 1))
                        pe.wait_ge(keys_out, t + 1)
                        for hd in range(H):
                            pe.matmul(ps[:, 4 * j + 3, hd * P:(hd + 1) * P], TT[:, j, hd], vb[:, t, hd],
                                      start=True, stop=True)
                            mm = pe.matmul(ps[:, 4 * j, hd * P:(hd + 1) * P], kbg[:, j, hd], TT[:, j, hd],
                                           start=True, stop=True)
                        mm.then_inc(uw_mm, 1)
                    for t in ts:
                        j = t % 2
                        pe.wait_ge(uw_out, t + 1)
                        pe.wait_ge(s_out, t + 1)
                        for hd in range(H):
                            mm = pe.matmul(ps[:, 4 * j + 1, hd * P:(hd + 1) * P], wT[:, j, hd], state[:, hd],
                                           start=True, stop=True)
                        mm.then_inc(p1_mm, 1)
                        pe.wait_ge(v_out, t + 1)
                        pe.wait_ge(qg_out, t + 1)
                        for hd in range(H):
                            w = slice(hd * P, (hd + 1) * P)
                            pe.matmul(ps[:, 4 * j + 3, w], kg[:, j, hd], v_new[:, j, hd], start=True, stop=True)
                            pe.matmul(ps[:, 4 * j + 2, w], qg[:, j, hd], state[:, hd], start=True, stop=False)
                            mm = pe.matmul(ps[:, 4 * j + 2, w], attnT[:, j, hd], v_new[:, j, hd], start=False, stop=True)
                        mm.then_inc(o_mm, 1)
                    for t in ts:
                        j = t % 2
                        pe.wait_ge(y_out, t + 1)
                        for hd in range(H):
                            mm = pe.transpose(ps[:, 4 * j, hd * P:(hd + 1) * P], o[:, j, hd], m.c(C_ID))
                        mm.then_inc(y_turned, 1)

            @block.vector
            def _(v):
                steps = Steps(v, s_dve)
                steps.link(v.memset(eps[:], NORM_EPS))
                v.memset(state, 0.0).then_inc(s_out, 1)
                v.wait_ge(summed, 1)
                v.tensor_copy(Gc[:].rearrange("p t h -> p (t h)"), ps[:, 0, 0:NT * H]).then_inc(gc_out, 1)
                v.wait_ge(bg_exp, 1)
                v.wait_ge(gc_out, 1)
                steps.link(v.tensor_tensor(bg[:], bg[:], beta[:], ALU.mult))
                for pair in range(NT // 2):
                    ts = (2 * pair, 2 * pair + 1)
                    for t in ts:
                        v.tensor_tensor(diag[:, t % 2], mat(C_ID), col(Gc[:, t]), ALU.mult).then_inc(diagd, 1)
                    for t in ts:
                        j = t % 2
                        v.wait_ge(gb, t + 1)
                        g = bank(4 * j)
                        steps.link(v.tensor_tensor(decay[:, j], g, col(Gc[:, t]), ALU.subtract))
                        v.tensor_tensor(kgs[:, j], g[:, :, P - 1], Gc[:, t], ALU.subtract)
                        v.tensor_scalar(decay[:, j], decay[:, j], 0.0, None, ALU.min).then_inc(diff, 1)
                    for t in ts:
                        j = t % 2
                        v.wait_ge(kk, t + 1)
                        v.wait_ge(masked, t + 1)
                        both = ps[:, 4 * j + 1:4 * j + 3, :].rearrange("p b (h a w) -> p (b h) a w", a=2, w=P)
                        v.tensor_tensor(AT[:, j], both[:, :, 0, :], decay[:, j], ALU.mult).then_inc(at_out, 1)
                        steps.link(v.tensor_tensor(attnT[:, j], both[:, :, 1, :], decay[:, j], ALU.mult))
                        v.wait_ge(k_turned, t + 1)
                        steps.link(v.tensor_tensor(kbg[:, j], bank(4 * j + 3), col(bg[:, t]), ALU.mult))
                        v.tensor_tensor(kg[:, j], bank(4 * j + 3), col(kgs[:, j]), ALU.mult).then_inc(keys_out, 1)
                    for l in range(L):
                        for t in ts:
                            j = t % 2
                            v.wait_ge(x_mm, lv(t, l))
                            v.tensor_tensor(X[:, j], bank(4 * j), col(beta[:, t]), ALU.mult).then_inc(x_out, 1)
                        for t in ts:
                            j = t % 2
                            v.wait_ge(tx_mm, lv(t, l))
                            if l == 0:
                                v.wait_ge(x_out, lv(t, l))
                                steps.link(v.tensor_tensor(T[:, j], mat(C_ID), X[:, j], ALU.subtract))
                                ins = v.tensor_tensor(TT[:, j], mat(C_ID), bank(4 * j + 2), ALU.subtract)
                            else:
                                if l < L - 1:
                                    steps.link(v.tensor_tensor(T[:, j], T[:, j], bank(4 * j + 1), ALU.subtract))
                                ins = v.tensor_tensor(TT[:, j], TT[:, j], bank(4 * j + 2), ALU.subtract)
                            ins.then_inc(t_out, 1)
                    for t in ts:
                        j = t % 2
                        v.wait_ge(p1_mm, t + 1)
                        v.tensor_tensor(v_new[:, j], u[:, j], bank(4 * j + 1), ALU.subtract).then_inc(v_out, 1)
                        v.wait_ge(o_mm, t + 1)
                        for hd in range(H):
                            ins = v.scalar_tensor_tensor(state[:, hd], state[:, hd], expg[:, j, hd, P - 1:P],
                                                         ps[:, 4 * j + 3, hd * P:(hd + 1) * P], ALU.mult, ALU.add)
                        ins.then_inc(s_out, 1)
                    for t in ts:
                        j = t % 2
                        v.wait_ge(rms_out, t + 1)
                        steps.link(v.reciprocal(ms[:, j], ms[:, j]))
                        steps.link(v.tensor_tensor(o[:, j], bank(4 * j + 2), col(ms[:, j]), ALU.mult))
                        norm_g = m.rows[:, None, R_NORM:R_NORM + P].to_broadcast([P, H, P])
                        steps.link(v.tensor_tensor(o[:, j], o[:, j], norm_g, ALU.mult))
                        v.tensor_tensor(o[:, j], o[:, j], z[:, t, :].rearrange("p (h w) -> p h w", w=P),
                                        ALU.mult).then_inc(y_out, 1)

            @block.scalar
            def _(act):
                steps = Steps(act, s_act)
                act.wait_ge(gc_out, 1)
                act.activation(bg[:], Gc[:], ACT.Exp).then_inc(bg_exp, 1)
                for pair in range(NT // 2):
                    ts = (2 * pair, 2 * pair + 1)
                    for t in ts:
                        j = t % 2
                        act.wait_ge(diff, t + 1)
                        act.activation(expg[:, j], bank(4 * j), ACT.Exp)
                        act.activation(kgs[:, j], kgs[:, j], ACT.Exp)
                        act.activation(decay[:, j], decay[:, j], ACT.Exp).then_inc(expd, 1)
                    for t in ts:
                        j = t % 2
                        act.wait_ge(uw_mm, t + 1)
                        act.activation(u[:, j], bank(4 * j + 3), ACT.Copy)
                        act.activation(wT[:, j], bank(4 * j), ACT.Copy).then_inc(uw_out, 1)
                    for t in ts:
                        j = t % 2
                        act.wait_ge(o_mm, t + 1)
                        for hd in range(H):
                            ins = act.activation(junk[:, j, hd], ps[:, 4 * j + 2, hd * P:(hd + 1) * P], ACT.Square,
                                                 accum_out=ms[:, j, hd:hd + 1])
                        ins.then_inc(squared, 1)
                    for t in ts:
                        j = t % 2
                        act.wait_ge(squared, t + 1)
                        act.activation(ms[:, j], ms[:, j], ACT.Sqrt, scale=1.0 / P, bias=eps[:, 0:1]).then_inc(rms_out, 1)
                    for t in ts:
                        act.wait_ge(y_turned, t + 1)
                        act.activation(hT[:, 4:8, span(t)], bank(4 * (t % 2)), ACT.Copy).then_inc(y_done, 1)

            @block.gpsimd
            def _(pool):
                for pair in range(NT // 2):
                    ts = (2 * pair, 2 * pair + 1)
                    for t in ts:
                        j = t % 2
                        pool.wait_ge(expd, t + 1)
                        pool.tensor_tensor(decay[:, j], decay[:, j], mat(C_UTRI), ALU.mult).then_inc(masked, 1)
                    for l in range(L):
                        for t in ts:
                            j = t % 2
                            pool.wait_ge(at_out, t + 1)
                            if l:
                                pool.wait_ge(x_mm, lv(t, l - 1))
                            pool.tensor_tensor(CT[:, j], AT[:, j], mat(C_LEVEL + l * P), ALU.mult).then_inc(ct_out, 1)
                        if l == 0:
                            for t in ts:
                                j = t % 2
                                pool.tensor_tensor(qg[:, j], bkq[:, 1, :, span(t)], expg[:, j], ALU.mult).then_inc(qg_out, 1)


def recurrent(m):
    nc, a, sb, sem, ps, hT = m.nc, m.a, m.sb, m.sem, m.ps, m.hT
    scope = ExitStack()
    with scope:
        w_ch = sb("rw_ch", [P, 2, KC, P], scope=scope)
        w_ax = sb("w_ax", [P, 2, 4, 2, 2 * P], scope=scope)
        vec = sb("rec_vec", [P, 8, KC], scope=scope)
        rate = sb("rate", [P, 6, KC], scope=scope)
        gate = sb("gelu", [P, KC, SEQ], scope=scope)
        xr = sb("xr", [P, KC, SEQ], scope=scope)
        raw = sb("rraw", [P, 2, CONV - 1 + SEQ], scope=scope)
        r = sb("r_gate", [P, 2, SEQ], scope=scope)
        i = sb("i_gate", [P, 2, SEQ], scope=scope)
        s_vec, s_ax, s_w = sem("vec_in"), sem("ax_in"), [sem(f"rw_in{j}") for j in range(2)]
        proj, evac, conv, zero = sem("r_proj"), sem("r_evac"), sem("r_conv"), sem("r_zero")
        s_dve, ax_mm, ax_out, decays, scanned = sem("r_dve"), sem("ax_mm"), sem("ax_out"), sem("r_decays"), sem("scanned")
        lam_in, lam_exp, rate_out, rooted, prepared = (sem(x) for x in ("lam_in", "lam_exp", "rate_out", "rooted", "prepared"))
        N = 2 * KC

        with nc.Block() as block:
            @block.sync
            def _(sp):
                sp.dma_start(vec[:], a["rec_vec"]).then_inc(s_vec, 16)
                for n in range(N):
                    if n >= 2:
                        sp.wait_ge(proj, n - 1)
                    sp.dma_start(w_ch[:, n % 2], a["rec_w_ch"][n]).then_inc(s_w[n % 2], 16)
                    if n == 3:
                        sp.dma_start(w_ax[:], a["w_ax"]).then_inc(s_ax, 16)

            @block.tensor
            def _(pe):
                for n in range(N):
                    pe.wait_ge(s_w[n % 2], 16 * (n // 2 + 1))
                    if n >= 2:
                        pe.wait_ge(evac, n - 1)
                    for hf in range(2):
                        for c in range(KC):
                            mm = pe.matmul(ps[:, 2 * (n % 2) + hf, :], w_ch[:, n % 2, c, :],
                                           hT[:, c, hf * HALF:(hf + 1) * HALF], start=(c == 0), stop=(c == KC - 1))
                    mm.then_inc(proj, 1)
                pe.wait_ge(s_ax, 16)
                for c in range(KC):
                    hd, q = c // 2, c % 2
                    pe.wait_ge(conv, KC)
                    for x in range(2):
                        k = 2 * c + x
                        if k >= 2:
                            pe.wait_ge(ax_out, k - 1)
                        for hf in range(2):
                            for kt in range(2):
                                mm = pe.matmul(ps[:, 4 + 2 * x + hf, :], w_ax[:, x, hd, kt, q * P:(q + 1) * P],
                                               xr[:, 2 * hd + kt, hf * HALF:(hf + 1) * HALF], start=(kt == 0), stop=(kt == 1))
                        mm.then_inc(ax_mm, 1)

            @block.scalar
            def _(act):
                act.wait_ge(lam_in, 1)
                act.activation(rate[:, 1, :], rate[:, 1, :], ACT.Exp, scale=-1.0).then_inc(lam_exp, 1)
                act.wait_ge(zero, 1)
                for n in range(N):
                    act.wait_ge(proj, n + 1)
                    src = ps[:, 2 * (n % 2):2 * (n % 2) + 2, :]
                    if n < KC:
                        if n >= 2:
                            act.wait_ge(conv, n - 1)
                        act.activation(raw[:, n % 2, CONV - 1:].rearrange("p (u f) -> p u f", u=2), src,
                                       ACT.Copy).then_inc(evac, 1)
                    else:
                        act.activation(gate[:, n - KC, :].rearrange("p (u f) -> p u f", u=2), src,
                                       ACT.Gelu_apprx_tanh).then_inc(evac, 1)
                act.wait_ge(rate_out, 1)
                for c in range(KC):
                    j = c % 2
                    for x, dst in enumerate((r, i)):
                        act.wait_ge(ax_mm, 2 * c + x + 1)
                        if c >= 2:
                            act.wait_ge(scanned, c - 1)
                        act.activation(dst[:, j, :].rearrange("p (u f) -> p u f", u=2), ps[:, 4 + 2 * x:6 + 2 * x, :],
                                       ACT.Sigmoid, bias=vec[:, 5 + x, c:c + 1]).then_inc(ax_out, 1)
                    act.wait_ge(ax_out, 2 * c + 2)
                    act.activation(raw[:, j, 0:SEQ], r[:, j, :], ACT.Tanh, scale=rate[:, 0, c:c + 1])
                    act.activation(r[:, j, :], r[:, j, :], ACT.Exp, scale=rate[:, 5, c:c + 1]).then_inc(decays, 1)
                    if c % 2:
                        for d in (c - 1, c):
                            act.wait_ge(prepared, d + 1)
                            act.activation(raw[:, d % 2, 0:SEQ], raw[:, d % 2, 0:SEQ], ACT.Sqrt).then_inc(rooted, 1)

            @block.vector
            def _(v):
                steps = Steps(v, s_dve)
                v.memset(raw[:, :, 0:CONV - 1], 0.0).then_inc(zero, 1)
                v.wait_ge(s_vec, 16)
                lam = vec[:, 7, :]
                steps.link(v.tensor_scalar(rate[:, 0, :], lam, -1.0, None, ALU.mult))
                v.tensor_tensor(rate[:, 1, :], lam, rate[:, 0, :], ALU.max).then_inc(lam_in, 1)
                v.wait_ge(lam_exp, 1)
                log1p_steps(v, steps, rate[:, 1, :], rate[:, 1, :], rate[:, 2, :], rate[:, 3, :], rate[:, 4, :])
                steps.link(v.scalar_tensor_tensor(rate[:, 0, :], rate[:, 0, :], 0.0, rate[:, 1, :], ALU.max, ALU.add))
                steps.link(v.tensor_scalar(rate[:, 0, :], rate[:, 0, :], 8.0, None, ALU.mult))
                v.tensor_scalar(rate[:, 5, :], rate[:, 0, :], -1.0, None, ALU.mult).then_inc(rate_out, 1)
                for n in range(KC):
                    v.wait_ge(evac, n + 1)
                    dst = xr[:, n, :]
                    steps.link(v.tensor_scalar(dst, raw[:, n % 2, 0:SEQ], vec[:, 0, n:n + 1], vec[:, 4, n:n + 1],
                                               ALU.mult, ALU.add))
                    for k in range(1, CONV):
                        ins = v.scalar_tensor_tensor(dst, raw[:, n % 2, k:k + SEQ], vec[:, k, n:n + 1], dst,
                                                     ALU.mult, ALU.add)
                        if k < CONV - 1:
                            steps.link(ins)
                    ins.then_inc(conv, 1)
                v.wait_ge(conv, KC)
                for c0 in range(0, KC, 2):
                    v.wait_ge(decays, c0 + 2)
                    for c in (c0, c0 + 1):
                        s, den, j = raw[:, c % 2, 0:SEQ], xr[:, c, :], c % 2
                        steps.link(v.tensor_tensor(i[:, j, :], i[:, j, :], xr[:, c, :], ALU.mult))
                        steps.link(v.tensor_scalar(den, s, 1.0, None, ALU.add))
                        steps.link(v.reciprocal(den, den))
                        v.scalar_tensor_tensor(s, s, 2.0, den, ALU.mult, ALU.mult).then_inc(prepared, 1)
                    for c in (c0, c0 + 1):
                        s, hc, j = raw[:, c % 2, 0:SEQ], xr[:, c, :], c % 2
                        v.wait_ge(rooted, c + 1)
                        steps.link(v.tensor_tensor(i[:, j, :], i[:, j, :], s, ALU.mult))
                        steps.link(v.tensor_tensor_scan(hc, r[:, j, :], i[:, j, :], 0.0, ALU.mult, ALU.add))
                        v.tensor_tensor(hT[:, c, :], gate[:, c, :], hc, ALU.mult).then_inc(scanned, 1)


def root_variance(act, stats, t, var_out, rooted):
    act.wait_ge(var_out, t + 1)
    act.activation(stats[:, 14:15], stats[:, 13:14], ACT.Sqrt, bias=stats[:, 15:16]).then_inc(rooted, 1)


def layer_norm_tile(m, v, steps, x, dst, stats, g_row, b_row, t, var_out, rooted):
    for k in range(2):
        steps.link(v.bn_stats(stats[:, 6 * k:6 * k + 6], x[:, k * HALF:(k + 1) * HALF]))
    v.bn_aggr(stats[:, 12:14], stats[:, 0:12]).then_inc(var_out, 1)
    v.wait_ge(rooted, t + 1)
    steps.link(v.reciprocal(stats[:, 14:15], stats[:, 14:15]))
    steps.link(v.tensor_scalar(x, x, stats[:, 12:13], stats[:, 14:15], ALU.subtract, ALU.mult))
    steps.link(v.tensor_tensor(x, x, g_row, ALU.mult))
    return v.tensor_tensor(dst, x, b_row, ALU.add)


def out_projection(m, layer, wgu, wd, w_sems):
    nc, a, sb, sem, ps, h, hT = m.nc, m.a, m.sb, m.sem, m.ps, m.h, m.hT
    scope = ExitStack()
    n_ = lambda x: f"{x}_o{layer}"
    with scope:
        w_out = sb(n_("w_out"), [P, KC, D], scope=scope)
        ln = wd[:, 1, 0:2, :]
        stats = sb(n_("stats"), [P, 16], scope=scope)
        s_w, s_ln, proj, ready, turned, out, stored, s_dve = (sem(n_(x)) for x in
            ("w_in", "ln_in", "proj", "h_ready", "turned", "ht_out", "h_stored", "dve"))
        var_out, rooted = sem(n_("var")), sem(n_("rooted"))
        with nc.Block() as block:
            @block.sync
            def _(sp):
                for q in range(4):
                    sp.dma_start(w_out[:, 2 * q:2 * q + 2, :], a["w_out"][layer][:, 2 * q:2 * q + 2, :]).then_inc(s_w, 16)
                sp.dma_start(ln, a["ln"][layer, 0].partition_broadcast(P)).then_inc(s_ln, 16)
                for e in range(2):
                    load_gate_up(sp, m, layer, e, e, wgu, w_sems)
                load_down(sp, m, layer, 0, 0, wd, w_sems)
                for t in range(NT):
                    sp.wait_ge(ready, t + 1)
                    sp.dma_start(m.h_dram[t * P:(t + 1) * P, :], h[:, t, :]).then_inc(stored, 16)
                sp.wait_ge(stored, 16 * NT)

            @block.tensor
            def _(pe):
                def turn(t):
                    pe.wait_ge(ready, t + 1)
                    if t >= 1:
                        pe.wait_ge(out, t)
                    for c in range(KC):
                        mm = pe.transpose(ps[:, 4 + c // 4, (c % 4) * P:(c % 4 + 1) * P], h[:, t, c::KC], m.c(C_ID))
                    mm.then_inc(turned, 1)

                pe.wait_ge(s_w, 64)
                for t in range(NT):
                    if t >= 2:
                        pe.wait_ge(ready, t - 1)
                    for hf in range(2):
                        for c in range(KC):
                            mm = pe.matmul(ps[:, 2 * (t % 2) + hf, :], hT[:, c, t * P:(t + 1) * P],
                                           w_out[:, c, hf * HALF:(hf + 1) * HALF], start=(c == 0), stop=(c == KC - 1))
                    mm.then_inc(proj, 1)
                    if t:
                        turn(t - 1)
                turn(NT - 1)

            @block.vector
            def _(v):
                steps = Steps(v, s_dve)
                steps.link(v.memset(stats[:, 15:16], LN_EPS))
                v.wait_ge(s_ln, 16)
                for t in range(NT):
                    v.wait_ge(proj, t + 1)
                    x = h[:, t, :]
                    steps.link(v.scalar_tensor_tensor(x.rearrange("p (u f) -> p u f", u=2), x.rearrange("p (u f) -> p u f", u=2),
                                                      ALPHA, ps[:, 2 * (t % 2):2 * (t % 2) + 2, :], ALU.mult, ALU.add))
                    layer_norm_tile(m, v, steps, x, x, stats, ln[:, 0, :], ln[:, 1, :], t, var_out, rooted).then_inc(ready, 1)

            @block.scalar
            def _(act):
                for t in range(NT + 1):
                    if t < NT:
                        root_variance(act, stats, t, var_out, rooted)
                    if t:
                        act.wait_ge(turned, t)
                        act.activation(hT[:, :, (t - 1) * P:t * P],
                                       ps[:, 4:6, :].rearrange("p b (c w) -> p (b c) w", w=P), ACT.Copy).then_inc(out, 1)


def load_gate_up(sp, m, layer, e, j, wgu, w_sems):
    for x, name in enumerate(("moe_w_gate", "moe_w_up")):
        w = m.a[name][layer, bass.ds(e, 1)].rearrange("e (p c) f -> p (e c) f", c=KC)
        sp.dma_start(wgu[:, j, x], w).then_inc(w_sems[x][j], 16)


def load_down(sp, m, layer, e, j, wd, w_sems):
    w = m.a["moe_w_down"][layer, bass.ds(e, 1)].rearrange("e (c p) d -> p (e c) d", c=FC)
    sp.dma_start(wd[:, j], w).then_inc(w_sems[2][j], 16)


def router(m, layer, wd, w_sems):
    nc, a, sb, sem, ps, hT, cst = m.nc, m.a, m.sb, m.sem, m.ps, m.hT, m.cst
    scope = ExitStack()
    n_ = lambda x: f"{x}_r{layer}"
    with scope:
        w = sb(n_("w_route"), [P, KC, ROUTES], scope=scope)
        lg = sb(n_("lg"), [P, NT, GROUPS], scope=scope)
        el = sb(n_("el"), [P, NT, EXPERTS], scope=scope)
        cand = sb(n_("cand"), [P, NT, EXPERTS], scope=scope)
        one = sb(n_("one"), [P, 2, NT, EXPERTS], scope=scope)
        both = sb(n_("both"), [P, NT, EXPERTS], scope=scope)
        g4 = sb(n_("g4"), [P, 2, NT, GROUPS], scope=scope)
        k = sb(n_("k"), [P, 20, NT], scope=scope)
        base = sb(n_("base"), [P, NT + 1, EXPERTS], scope=scope)
        ov = sb(n_("ov"), [P, 4, EXPERTS], scope=scope)
        tmp = sb(n_("tmp"), [P, 2, EXPERTS], scope=scope)
        slot = sb(n_("slot"), [P, 2, NT, P], scope=scope)
        blk = sb(n_("blk"), [P, 2, NT, TABLE], scope=scope)
        tab = sb(n_("tab"), [P, 3, TABLE], scope=scope)
        cnt = sb(n_("cnt"), [1, TABLE - EXPERTS, EXPERTS], scope=scope)
        ids = sb(n_("ids"), [1, TABLE + 1], scope=scope)
        s_w, logits, s_exp, exp_out, onehots, prefixed, s_dve, assigned, tabled, gs_exp = (sem(n_(x)) for x in
            ("w_in", "logits", "exp_in", "exp_out", "onehots", "prefixed", "dve", "assigned", "tabled", "gs_exp"))
        with nc.Block() as block:
            @block.sync
            def _(sp):
                sp.dma_start(w[:], a["w_route"][layer]).then_inc(s_w, 16)
                load_down(sp, m, layer, 1, 1, wd, w_sems)

            @block.tensor
            def _(pe):
                pe.wait_ge(s_w, 16)
                for t in range(NT):
                    for c in range(KC):
                        mm = pe.matmul(ps[:, 0, t * ROUTES:(t + 1) * ROUTES], hT[:, c, t * P:(t + 1) * P], w[:, c, :],
                                       start=(c == 0), stop=(c == KC - 1))
                mm.then_inc(logits, 1)
                pe.wait_ge(onehots, 1)
                flat = both[:].rearrange("p t e -> p (t e)")
                pe.matmul(ps[:, 1, 0:NT * EXPERTS], m.c(C_USTRICT), flat, start=True, stop=True)
                pe.matmul(ps[:, 2, 0:NT * EXPERTS], m.c(C_ONES), flat, start=True, stop=True).then_inc(prefixed, 1)
                pe.wait_ge(assigned, 1)
                for x in range(2):
                    for t in range(NT):
                        mm = pe.matmul(ps[:, 3, 0:TABLE], slot[:, x, t, :], blk[:, x, t, :],
                                       start=(x + t == 0), stop=(x == 1 and t == NT - 1))
                mm.then_inc(tabled, 1)

            @block.scalar
            def _(act):
                act.wait_ge(s_exp, 1)
                act.activation(g4[:, 1], g4[:, 1], ACT.Exp).then_inc(exp_out, 1)
                act.wait_ge(s_exp, 2)
                act.activation(k[:, 5, :], k[:, 5, :], ACT.Exp).then_inc(exp_out, 1)

            @block.vector
            def _(v):
                steps = Steps(v, s_dve)
                link = steps.link
                bc = lambda x, n: x[:, :, None].to_broadcast([P, NT, n])
                iota = lambda n: cst[:, None, C_IOTA:C_IOTA + n].to_broadcast([P, NT, n])
                rt = R_ROUTE + layer * ROUTES

                def first_of_largest(index, largest, values, scratch, n):
                    link(v.tensor_reduce(largest, values, AX, ALU.max))
                    link(v.tensor_tensor(scratch, values, bc(largest, n), ALU.is_ge))
                    link(v.scalar_tensor_tensor(scratch, scratch, -100.0, iota(n), ALU.mult, ALU.add))
                    link(v.tensor_reduce(index, scratch, AX, ALU.min))
                    link(v.tensor_scalar(index, index, 100.0, None, ALU.add))

                v.wait_ge(logits, 1)
                raw = ps[:, 0, 0:NT * ROUTES].rearrange("p (t r) -> p t r", r=ROUTES)
                link(v.tensor_tensor(lg[:], raw[:, :, 0:GROUPS],
                                     m.rows[:, None, rt:rt + GROUPS].to_broadcast([P, NT, GROUPS]), ALU.add))
                link(v.tensor_tensor(el[:], raw[:, :, GROUPS:],
                                     m.rows[:, None, rt + GROUPS:rt + ROUTES].to_broadcast([P, NT, EXPERTS]), ALU.add))
                first_of_largest(k[:, 1, :], k[:, 0, :], lg[:], g4[:, 0], GROUPS)
                v.tensor_tensor(g4[:, 1], lg[:], bc(k[:, 0, :], GROUPS), ALU.subtract).then_inc(s_exp, 1)
                link(v.tensor_tensor(g4[:, 0], iota(GROUPS), bc(k[:, 1, :], GROUPS), ALU.is_equal))
                link(v.tensor_scalar(g4[:, 0], g4[:, 0], 1.0, 1e30, ALU.subtract, ALU.mult))
                eg = el[:].rearrange("p t (g j) -> p (t g) j", j=PER_GROUP)
                link(v.tensor_tensor(eg, eg, g4[:, 0].rearrange("p t g -> p (t g)")[:, :, None]
                                     .to_broadcast([P, NT * GROUPS, PER_GROUP]), ALU.add))
                for x in range(2):
                    first_of_largest(k[:, 6 + x, :], k[:, 3 + x, :], el[:], cand[:], EXPERTS)
                    link(v.tensor_tensor(one[:, x], iota(EXPERTS), bc(k[:, 6 + x, :], EXPERTS), ALU.is_equal))
                    if x == 0:
                        link(v.scalar_tensor_tensor(el[:], one[:, 0], -2e30, el[:], ALU.mult, ALU.add))
                v.tensor_tensor(both[:], one[:, 0], one[:, 1], ALU.add).then_inc(onehots, 1)
                v.tensor_tensor(k[:, 5, :], k[:, 4, :], k[:, 3, :], ALU.subtract).then_inc(s_exp, 1)
                v.wait_ge(exp_out, 2)
                link(v.tensor_reduce(k[:, 2, :], g4[:, 1], AX, ALU.add))
                link(v.tensor_scalar(k[:, 8, :], k[:, 5, :], 1.0, None, ALU.add))
                link(v.tensor_tensor(k[:, 2, :], k[:, 2, :], k[:, 8, :], ALU.mult))
                link(v.reciprocal(m.gates[:, 0, :], k[:, 2, :]))
                link(v.tensor_tensor(m.gates[:, 1, :], m.gates[:, 0, :], k[:, 5, :], ALU.mult))
                v.wait_ge(prefixed, 1)
                within = ps[:, 1, 0:NT * EXPERTS].rearrange("p (t e) -> p t e", e=EXPERTS)
                totals = ps[:, 2, 0:NT * EXPERTS].rearrange("p (t e) -> p t e", e=EXPERTS)
                link(v.memset(base[:, 0, :], 0.0))
                for t in range(NT):
                    link(v.tensor_tensor(base[:, t + 1, :], base[:, t, :], totals[:, t, :], ALU.add))
                link(v.tensor_tensor(both[:], base[:, 0:NT, :], within, ALU.add))
                count = base[:, NT, :]
                link(v.tensor_scalar(ov[:, 0, :], count, float(P), None, ALU.is_gt))
                for q in range(2, NT):
                    link(v.scalar_tensor_tensor(ov[:, 0, :], count, float(P * q), ov[:, 0, :], ALU.is_gt, ALU.add))
                link(v.memset(tmp[:, 0, :], 1.0))
                link(v.tensor_tensor_scan(ov[:, 1, :], tmp[:, 0, :], ov[:, 0, :], 0.0, ALU.mult, ALU.add))
                link(v.tensor_tensor(ov[:, 2, :], ov[:, 1, :], ov[:, 0, :], ALU.subtract))
                exov = ov[:, 2:3, :].to_broadcast([P, NT, EXPERTS])
                for x in range(2):
                    e, rank, first, hi, bl = (k[:, 6 + x, :], k[:, 9, :], k[:, 10, :], k[:, 11, :], k[:, 12, :])
                    link(v.tensor_tensor(cand[:], one[:, x], both[:], ALU.mult))
                    link(v.tensor_reduce(rank, cand[:], AX, ALU.add))
                    link(v.tensor_tensor(cand[:], one[:, x], exov, ALU.mult))
                    link(v.tensor_reduce(first, cand[:], AX, ALU.add))
                    link(v.tensor_scalar(hi, rank, float(P), None, ALU.is_ge))
                    for q in range(2, NT):
                        link(v.scalar_tensor_tensor(hi, rank, float(P * q), hi, ALU.is_ge, ALU.add))
                    link(v.tensor_tensor(bl, first, hi, ALU.add))
                    link(v.scalar_tensor_tensor(bl, bl, float(EXPERTS - 1), e, ALU.add, ALU.subtract))
                    link(v.tensor_scalar(first, hi, 1.0, None, ALU.min))
                    link(v.tensor_tensor(bl, bl, first, ALU.mult))
                    link(v.tensor_tensor(bl, bl, e, ALU.add))
                    link(v.scalar_tensor_tensor(rank, hi, -float(P), rank, ALU.mult, ALU.add))
                    link(v.tensor_tensor(slot[:, x], iota(P), bc(rank, P), ALU.is_equal))
                    link(v.tensor_tensor(blk[:, x], iota(TABLE), bc(bl, TABLE), ALU.is_equal))
                    link(v.tensor_scalar(k[:, 13, :], cst[:, C_TOKEN:C_TOKEN + NT], float(SEQ * x), None, ALU.add))
                    ins = v.tensor_tensor(blk[:, x], blk[:, x], bc(k[:, 13, :], TABLE), ALU.mult)
                    if x == 0:
                        link(ins)
                    else:
                        ins.then_inc(assigned, 1)
                inc = ov[0:1, 1, :]
                nb = TABLE - EXPERTS
                link(v.tensor_tensor(cnt[:], inc[:, None, :].to_broadcast([1, nb, EXPERTS]),
                                     cst[0:1, C_IOTA:C_IOTA + nb, None].to_broadcast([1, nb, EXPERTS]), ALU.is_le))
                link(v.tensor_reduce(ids[:, EXPERTS:TABLE], cnt[:], AX, ALU.add))
                link(v.tensor_scalar(ids[:, EXPERTS:TABLE], ids[:, EXPERTS:TABLE], float(EXPERTS - 1), None, ALU.min))
                link(v.tensor_copy(ids[:, 0:EXPERTS], cst[0:1, C_IOTA:C_IOTA + EXPERTS]))
                link(v.tensor_scalar(tmp[0:1, 0, 0:8], cst[0:1, C_STEP:C_STEP + 8], inc[:, EXPERTS - 1:EXPERTS], None, ALU.is_lt))
                link(v.tensor_reduce(ids[:, TABLE:], tmp[0:1, 0, 0:8], AX, ALU.add))
                link(v.tensor_scalar(ids[:, TABLE:], ids[:, TABLE:], float(EXPERTS // 2), None, ALU.add))
                link(v.tensor_copy(m.ctl[:], ids[:]))
                v.wait_ge(tabled, 1)
                val, none, row = tab[:, 0, :], tab[:, 1, :], tab[:, 2, :]
                link(v.tensor_copy(val, ps[:, 3, 0:TABLE]))
                link(v.tensor_scalar(none, val, 0.0, float(NOBODY), ALU.is_equal, ALU.mult))
                link(v.scalar_tensor_tensor(row, val, -1.0, none, ALU.add, ALU.add))
                link(v.tensor_copy(m.dst_idx[:], row))
                link(v.tensor_scalar(val, val, float(SEQ), -float(SEQ), ALU.is_gt, ALU.mult))
                link(v.tensor_tensor(row, row, val, ALU.add))
                link(v.tensor_copy(m.src_idx[:], row))


def expert_blocks(m, layer, wgu, wd, w_sems):
    nc, a, sb, sem, ps, cst = m.nc, m.a, m.sb, m.sem, m.ps, m.cst
    scope = ExitStack()
    n_ = lambda x: f"{x}_e{layer}"
    with scope:
        x = sb(n_("x"), [P, 2, D], scope=scope)
        xT = sb(n_("xT"), [P, KC, P], scope=scope)
        act_g = sb(n_("act_g"), [P, F], scope=scope)
        hid = sb(n_("hid"), [P, F], scope=scope)
        hidT = sb(n_("hidT"), [P, FC, P], scope=scope)
        y = sb(n_("y"), [P, 2, D], scope=scope)
        idx = sb(n_("idx"), [P, 2, 2], I32, scope=scope)
        (ready0, x_free, x_turned, x_out, gated, silu, upped, hid_out, h_turned, h_out, downed, y_out,
         idx_src, idx_dst) = (sem(n_(s)) for s in
            ("x_zero", "x_free", "x_turned", "x_out", "gated", "silu", "upped", "hid_out", "h_turned", "h_out",
             "downed", "y_out", "idx_src", "idx_dst"))
        cleared = sem(n_("dma_cleared_to_go"))
        gathered = [sem(n_(f"gathered{j}")) for j in range(2)]
        scattered = [sem(n_(f"scattered{j}")) for j in range(2)]

        def turns(eng):
            return eng.value_load(m.ctl[0:1, TABLE:TABLE + 1], min_val=EXPERTS // 2, max_val=BLOCKS // 2)

        with nc.Block() as block:
            @block.sync
            def _(sp):
                n = turns(sp)
                with sp.Fori(0, n - 1) as i:
                    for j in range(2):
                        e = sp.value_load(m.ctl[0:1, bass.ds(2 * i + 2 + j, 1)], min_val=0, max_val=EXPERTS - 1)
                        sp.wait_ge(upped, 2 * (2 * i + j) + 2)
                        load_gate_up(sp, m, layer, e, j, wgu, w_sems)
                        sp.wait_ge(downed, 2 * i + j + 1)
                        load_down(sp, m, layer, e, j, wd, w_sems)

            @block.gpsimd
            def _(pool):
                pool.memset(x[:], 0.0).then_inc(ready0, 1)
                pool.memset(idx[:], 0).then_inc(ready0, 1)
                pool.wait_ge(ready0, 2)
                for j in range(2):
                    pool.dma_start(m.scratch[j], idx[:, j, :]).then_inc(scattered[j], 16)
                for j in range(2):
                    pool.wait_ge(scattered[j], 16)
                pool.wait_ge(ready0, 1)

                last_token, last_row = pool.to_reg(SEQ - 1), pool.to_reg(2 * SEQ - 1)

                def gather(b, j, turn, free, last):
                    if free is not None:
                        pool.wait_ge(gathered[j], last)
                    pool.tensor_copy(idx[:, j, 0:1], m.src_idx[:, bass.ds(b, 1)]).then_inc(idx_src, 1)
                    pool.wait_ge(idx_src, turn)
                    if free is not None:
                        pool.wait_ge(x_turned, free)
                    pool.sem_inc(cleared, 1)
                    pool.indirect_dma_start(x[:, j, :], None, m.h_dram, bass.IndirectOffsetOnAxis(ap=idx[:, j, 0:1], axis=0),
                                            bounds_check=last_token, oob_is_err=False).then_inc(gathered[j], 16)

                def scatter(b, j, turn, last):
                    pool.wait_ge(scattered[j], last)
                    pool.tensor_copy(idx[:, j, 1:2], m.dst_idx[:, bass.ds(b, 1)]).then_inc(idx_dst, 1)
                    pool.wait_ge(idx_dst, turn)
                    pool.wait_ge(y_out, turn)
                    pool.sem_inc(cleared, 1)
                    pool.indirect_dma_start(m.y_dram, bass.IndirectOffsetOnAxis(ap=idx[:, j, 1:2], axis=0), y[:, j, :], None,
                                            bounds_check=last_row, oob_is_err=False).then_inc(scattered[j], 16)

                gather(0, 0, 1, None, None)
                gather(1, 1, 2, None, None)
                n = turns(pool)
                with pool.Fori(0, n) as i:
                    for j in range(2):
                        gather(2 * i + 2 + j, j, 2 * i + 3 + j, 2 * i + 1 + j, 16 * i + 16)
                        scatter(2 * i + j, j, 2 * i + 1 + j, 16 * i + 16)
                for j in range(2):
                    pool.wait_ge(scattered[j], n * 16 + 16)
                    pool.wait_ge(gathered[j], n * 16 + 16)

            @block.tensor
            def _(pe):
                def turn_x(b, j, k):
                    pe.wait_ge(gathered[j], k)
                    for c in range(KC):
                        mm = pe.transpose(ps[:, c // 4, (c % 4) * P:(c % 4 + 1) * P], x[:, j, c::KC], m.c(C_ID))
                    mm.then_inc(x_turned, 1)

                turn_x(0, 0, 16)
                n = turns(pe)
                with pe.Fori(0, n) as i:
                    for j in range(2):
                        b = 2 * i + j
                        pe.wait_ge(x_out, b + 1)
                        pe.wait_ge(w_sems[0][j], 16 * i + 16)
                        for c in range(KC):
                            mm = pe.matmul(ps[:, 2, :], xT[:, c, :], wgu[:, j, 0, c, :], start=(c == 0), stop=(c == KC - 1))
                        mm.then_inc(gated, 1)
                        pe.wait_ge(w_sems[1][j], 16 * i + 16)
                        for q in range(2):
                            for c in range(KC):
                                mm = pe.matmul(ps[:, 3 + q, 0:F // 2], xT[:, c, :], wgu[:, j, 1, c, q * (F // 2):(q + 1) * (F // 2)],
                                               start=(c == 0), stop=(c == KC - 1))
                            mm.then_inc(upped, 1)
                        turn_x(b + 1, 1 - j, 16 * i + 16 if j == 0 else 16 * i + 32)
                        for q in range(2):
                            pe.wait_ge(hid_out, 2 * b + 1 + q)
                            for c in range(2 * q, 2 * q + 2):
                                mm = pe.transpose(ps[:, 5 - 3 * q, c * P:(c + 1) * P], hid[:, c * P:(c + 1) * P], m.c(C_ID))
                            mm.then_inc(h_turned, 1)
                        pe.wait_ge(w_sems[2][j], 16 * i + 16)
                        pe.wait_ge(h_out, 2 * b + 2)
                        for hf in range(2):
                            for c in range(FC):
                                mm = pe.matmul(ps[:, 6 + hf, :], hidT[:, c, :], wd[:, j, c, hf * HALF:(hf + 1) * HALF],
                                               start=(c == 0), stop=(c == FC - 1))
                        mm.then_inc(downed, 1)

            @block.scalar
            def _(act):
                def copy_x(b):
                    act.wait_ge(x_turned, b + 1)
                    act.activation(xT[:].rearrange("p c w -> p (c w)"), ps[:, 0:2, :].rearrange("p b f -> p (b f)"),
                                   ACT.Copy).then_inc(x_out, 1)

                copy_x(0)
                n = turns(act)
                with act.Fori(0, n) as i:
                    for j in range(2):
                        b = 2 * i + j
                        act.wait_ge(gated, b + 1)
                        act.activation(act_g[:], ps[:, 2, :], ACT.Silu).then_inc(silu, 1)
                        copy_x(b + 1)
                        act.wait_ge(scattered[j], 16 * i + 16)
                        act.wait_ge(downed, b + 1)
                        act.activation(y[:, j, :], ps[:, 6:8, :].rearrange("p b f -> p (b f)"), ACT.Copy).then_inc(y_out, 1)

            @block.vector
            def _(v):
                n = turns(v)
                with v.Fori(0, n) as i:
                    for j in range(2):
                        b = 2 * i + j
                        v.wait_ge(silu, b + 1)
                        for q in range(2):
                            cols = slice(q * (F // 2), (q + 1) * (F // 2))
                            v.wait_ge(upped, 2 * b + q + 1)
                            v.tensor_tensor(hid[:, cols], act_g[:, cols], ps[:, 3 + q, 0:F // 2], ALU.mult).then_inc(hid_out, 1)
                        for q in range(2):
                            v.wait_ge(h_turned, 2 * b + q + 1)
                            v.tensor_copy(hidT[:, 2 * q:2 * q + 2, :],
                                          ps[:, 5 - 3 * q, 2 * q * P:(2 * q + 2) * P].rearrange("p (c w) -> p c w", w=P)).then_inc(h_out, 1)


def combine(m, layer, out):
    nc, a, sb, sem, ps, h, hT = m.nc, m.a, m.sb, m.sem, m.ps, m.h, m.hT
    scope = ExitStack()
    n_ = lambda x: f"{x}_c{layer}"
    with scope:
        ln = sb(n_("ln"), [P, 2, D], scope=scope)
        y = sb(n_("y"), [P, 4, 2, D], scope=scope)
        stats = sb(n_("stats"), [P, 16], scope=scope)
        s_y = [sem(n_(f"y_in{q}")) for q in range(4)]
        s_ln, ready, turned, copied, stored, s_dve = (sem(n_(x)) for x in
            ("ln_in", "h_ready", "turned", "ht_out", "stored", "dve"))
        var_out, rooted = sem(n_("var")), sem(n_("rooted"))
        with nc.Block() as block:
            @block.sync
            def _(sp):
                sp.dma_start(ln[:], a["ln"][layer, 1].partition_broadcast(P)).then_inc(s_ln, 16)
                rows = m.y_dram.rearrange("(k t p) d -> t p k d", k=2, p=P)
                for t in range(NT):
                    if t >= 4:
                        sp.wait_ge(ready, t - 3)
                    sp.dma_start(y[:, t % 4], rows[t]).then_inc(s_y[t % 4], 16)
                    if out is not None and t >= 3:
                        sp.wait_ge(ready, t - 2)
                        sp.dma_start(out[0, (t - 3) * P:(t - 2) * P, :], h[:, t - 3, :]).then_inc(stored, 16)
                if out is not None:
                    for t in range(NT - 3, NT):
                        sp.wait_ge(ready, t + 1)
                        sp.dma_start(out[0, t * P:(t + 1) * P, :], h[:, t, :]).then_inc(stored, 16)
                    sp.wait_ge(stored, 16 * NT)

            @block.vector
            def _(v):
                steps = Steps(v, s_dve)
                steps.link(v.memset(stats[:, 15:16], LN_EPS))
                v.wait_ge(s_ln, 16)
                for t in range(NT):
                    x = h[:, t, :]
                    v.wait_ge(s_y[t % 4], 16 * (t // 4 + 1))
                    steps.link(v.tensor_scalar(x, x, ALPHA, None, ALU.mult))
                    for k in range(2):
                        steps.link(v.scalar_tensor_tensor(x, y[:, t % 4, k, :], m.gates[:, k, t:t + 1], x, ALU.mult, ALU.add))
                    layer_norm_tile(m, v, steps, x, x, stats, ln[:, 0, :], ln[:, 1, :], t, var_out, rooted).then_inc(ready, 1)

            @block.tensor
            def _(pe):
                for t in range(NT if out is None else 0):
                    pe.wait_ge(ready, t + 1)
                    if t >= 2:
                        pe.wait_ge(copied, t - 1)
                    for c in range(KC):
                        mm = pe.transpose(ps[:, 2 * (t % 2) + c // 4, (c % 4) * P:(c % 4 + 1) * P], h[:, t, c::KC], m.c(C_ID))
                    mm.then_inc(turned, 1)

            @block.scalar
            def _(act):
                for t in range(NT + 1):
                    if t < NT:
                        root_variance(act, stats, t, var_out, rooted)
                    if t and out is None:
                        act.wait_ge(turned, t)
                        act.activation(hT[:, :, (t - 1) * P:t * P],
                                       ps[:, 2 * ((t - 1) % 2):2 * ((t - 1) % 2) + 2, :].rearrange("p b (c w) -> p (b c) w", w=P),
                                       ACT.Copy).then_inc(copied, 1)


def lay_out(x, positions, hyb_w_in, hyb_sinks, hyb_conv_w, hyb_a_log, hyb_dt_bias, hyb_norm_g,
            hyb_w_out, rec_w_in, rec_conv_w, rec_conv_b, rec_w_a, rec_b_a, rec_w_x, rec_b_x,
            rec_lambda, rec_w_out, moe_rg_w, moe_rg_b, moe_re_w, moe_re_b, moe_w_gate, moe_w_up,
            moe_w_down, ln_g, ln_b):
    def by_row(w):
        return w.reshape(P, KC, w.shape[-1])

    def tiles(w):
        return by_row(w).reshape(P, KC, -1, P).transpose(2, 0, 1, 3)

    w = hyb_w_in[0]
    q = w[:, 0:512].reshape(D, 2, 4, A_HD).transpose(0, 2, 1, 3).reshape(D, 512)
    ch = np.concatenate([q, w[:, 512:640], w[:, 768:2304]], axis=1)
    cols = lambda v: v.reshape(KC, P).T
    rec = rec_w_in[0]
    out = {
        "x": x[0],
        "xT": by_row(x[0].T),
        "positions": positions[0],
        "cst": constants(),
        "rows": np.concatenate([hyb_sinks[0], hyb_a_log[0], hyb_dt_bias[0], hyb_norm_g[0],
                                moe_rg_b[0], moe_re_b[0], moe_rg_b[1], moe_re_b[1]]),
        "w_ch": tiles(ch),
        "w_vs": by_row(np.concatenate([w[:, 640:768], w[:, 2816:2824]], axis=1)),
        "w_z": by_row(w[:, 2304:2816]),
        "conv_w": hyb_conv_w[0].T.reshape(12, P, CONV).transpose(1, 0, 2),
        "w_out": np.stack([hyb_w_out[0], rec_w_out[0]]).reshape(2, KC, P, D).transpose(0, 2, 1, 3),
        "rec_w_ch": tiles(np.concatenate([rec[:, D:], rec[:, :D]], axis=1)),
        "rec_vec": np.stack([cols(v) for v in (*rec_conv_w[0], rec_conv_b[0], rec_b_a[0], rec_b_x[0], rec_lambda[0])], axis=1),
        "w_ax": np.stack([rec_w_a[0], rec_w_x[0]]).reshape(2, 4, 2, P, 2 * P).transpose(3, 0, 1, 2, 4),
        "w_route": np.concatenate([moe_rg_w, moe_re_w], axis=2).reshape(2, P, KC, ROUTES),
        "moe_w_gate": moe_w_gate,
        "moe_w_up": moe_w_up,
        "moe_w_down": moe_w_down,
        "ln": np.stack([ln_g, ln_b], axis=2),
    }
    return {k: np.ascontiguousarray(v) for k, v in out.items()}


def kernel(stop=None, **inputs):
    from concourse import bacc
    from concourse.bass_utils import run_bass_kernel_spmd

    arrays = lay_out(**{k: np.asarray(v) for k, v in inputs.items()})
    nc = bacc.Bacc("TRN2", target_bir_lowering=False, num_devices=1)
    a = {k: nc.dram_tensor(f"in_{k}", v.shape, mybir.dt.from_np(v.dtype), kind="ExternalInput").ap() for k, v in arrays.items()}
    out = nc.dram_tensor("out", (1, SEQ, D), F32, kind="ExternalOutput").ap()
    program(nc, a, out, stop)
    r = run_bass_kernel_spmd(nc, [{f"in_{k}": v for k, v in arrays.items()}], core_ids=[0])
    return r.results[0]["out"]
```

```python
from contextlib import ExitStack

import numpy as np

import concourse.bass as bass
from concourse import mybir
from concourse.alu_op_type import AluOpType as ALU

ACT = mybir.ActivationFunctionType
F32 = mybir.dt.float32
F32R = mybir.dt.float32r
I32 = mybir.dt.int32
AX = mybir.AxisListType.X

P = 128
SEQ = 1024
D = 1024
NT = SEQ // P
KC = D // P
HALF = 512

A_HEADS, A_KV, A_HD = 8, 2, 64
B_HEADS = 4
CONV = 4
WIN = 2 * P
THETA = 10000.0
NORM_EPS, LN_EPS = 1e-6, 1e-5
ALPHA = 4.0 ** 0.25

GROUPS, PER_GROUP = 4, 8
EXPERTS = GROUPS * PER_GROUP
ROUTES = GROUPS + EXPERTS
F = 512
FC = F // P
OVERFLOW = 16
BLOCKS = EXPERTS + OVERFLOW
TABLE = BLOCKS + 2
NOBODY = 1 << 20

PIECES = 6
PIECE = 2048
RING = 4

LEVELS = 7
N_CH = 17
N_QK = 5

C_ID, C_UTRI, C_USTRICT, C_ONES = 0, P, 2 * P, 3 * P
C_LEVEL = 4 * P
C_AMASK = C_LEVEL + LEVELS * P
C_PERM = C_AMASK + WIN
C_IOTA = C_PERM + P
C_INV = C_IOTA + P
C_TOKEN = C_INV + 1
C_STEP = C_TOKEN + 2 * NT
N_CONST = C_STEP + 8

R_SINK, R_ALOG, R_DT, R_NORM = 0, 8, 12, 16
R_ROUTE = 16 + P
N_ROW = R_ROUTE + 2 * ROUTES


def constants():
    c = np.zeros((P, N_CONST), np.float32)
    p = np.arange(P)
    i, j = p[:, None], p[None, :]
    c[:, C_ID:C_ID + P] = i == j
    c[:, C_UTRI:C_UTRI + P] = i <= j
    c[:, C_USTRICT:C_USTRICT + P] = i < j
    c[:, C_ONES:C_ONES + P] = 1.0
    for level in range(LEVELS):
        s = 1 << level
        m = (i // (2 * s) == j // (2 * s)) & ((j // s) % 2 == 1) & ((i // s) % 2 == 0)
        c[:, C_LEVEL + level * P:C_LEVEL + (level + 1) * P] = m
    key = np.arange(WIN)[None, :]
    first = (i < P // 2) & (key >= P // 2) & (key < 3 * P // 2)
    second = (i >= P // 2) & (key >= P)
    c[:, C_AMASK:C_AMASK + WIN] = np.where(first | second, 0.0, -1e30)
    half = A_HD // 2
    for d in range(P):
        if d % A_HD < half:
            c[d + half, C_PERM + d] = -1.0
        else:
            c[d - half, C_PERM + d] = 1.0
    c[:, C_IOTA:C_IOTA + P] = j
    inv = np.float32(THETA) ** (-np.arange(half, dtype=np.float32) / np.float32(half))
    c[:, C_INV] = inv[p % half]
    for t in range(2 * NT):
        c[:, C_TOKEN + t] = t * P + p + 1
    c[:, C_STEP:C_STEP + 8] = 2 * np.arange(8)
    return c


class Steps:

    def __init__(self, eng, sem, base=0):
        self.eng, self.sem, self.base, self.n = eng, sem, base, 0

    def link(self, ins):
        self.n += 1
        ins.then_inc(self.sem, 1)
        self.eng.wait_ge(self.sem, self.base + self.n)


def program(nc, a, out):
    ctx = ExitStack()
    with ctx:
        def sb(name, shape, dt=F32, scope=ctx):
            return scope.enter_context(nc.sbuf_tensor(name, shape, dt))

        def sb_both(name, shape, scope=ctx):
            with ExitStack() as passing:
                plain = sb(name, shape, scope=passing)
            return plain, sb(name + "_r", shape, F32R, scope=scope)

        stage_sems = []

        def sem(name):
            stage_sems.append(nc.alloc_semaphore(name))
            return stage_sems[-1]

        def end_stage():
            nc.clear_and_free_semaphores(list(stage_sems))
            nc.all_engine_barrier()
            stage_sems.clear()

        h_dram = nc.dram_tensor("h_rows", (SEQ, D), F32, kind="Internal").ap()
        y_dram = nc.dram_tensor("expert_rows", (2 * SEQ, D), F32, kind="Internal").ap()

        ps = ctx.enter_context(nc.psum_tensor("ps", [P, 8, HALF], F32))
        h, h_r = sb_both("h", [P, NT, D])
        hT, hT_r = sb_both("hT", [P, KC, SEQ])
        cst = sb("cst", [P, N_CONST])
        rows = sb("rows", [P, N_ROW])
        gates = sb("gates", [P, 2, NT])
        src_idx = sb("src_idx", [P, TABLE], I32)
        dst_idx = sb("dst_idx", [P, TABLE], I32)
        ctl = sb("ctl", [1, TABLE + 1], I32)

        m = Machine(nc, a, sb, sb_both, sem, ps, h, h_r, hT, hT_r, cst, rows, gates, src_idx, dst_idx, ctl, h_dram, y_dram)
        hybrid(m)
        end_stage()
        for layer in range(2):
            if layer == 1:
                recurrent(m)
            experts = ExitStack()
            with experts:
                raw = sb(f"raw{layer}", [P, RING - 1, PIECE], scope=experts)
                landed = [sem(f"landed{layer}{slot}") for slot in range(RING)]
                out_projection(m, layer, raw, landed)
                router(m, layer)
                expert_blocks(m, layer, raw, landed)
            combine(m, layer, out if layer == 1 else None)
            end_stage()


class Machine:

    def __init__(self, nc, a, sb, sb_both, sem, ps, h, h_r, hT, hT_r, cst, rows, gates, src_idx, dst_idx, ctl, h_dram, y_dram):
        self.nc, self.a, self.sb, self.sem = nc, a, sb, sem
        self.sb_both, self.h_r, self.hT_r = sb_both, h_r, hT_r
        self.ps, self.h, self.hT, self.cst, self.rows = ps, h, hT, cst, rows
        self.gates, self.src_idx, self.dst_idx, self.ctl = gates, src_idx, dst_idx, ctl
        self.h_dram, self.y_dram = h_dram, y_dram

    def c(self, at, n=P):
        return self.cst[:, at:at + n]


def log1p_steps(v, steps, out, e, z, z2, poly):
    terms = 8
    steps.link(v.tensor_scalar(z, e, 2.0, None, ALU.add))
    steps.link(v.reciprocal(z, z))
    steps.link(v.tensor_tensor(z, e, z, ALU.mult))
    steps.link(v.tensor_tensor(z2, z, z, ALU.mult))
    steps.link(v.tensor_scalar(poly, z2, 1.0 / (2 * terms + 1), 1.0 / (2 * terms - 1), ALU.mult, ALU.add))
    for n in range(terms - 2, -1, -1):
        steps.link(v.tensor_tensor(poly, poly, z2, ALU.mult))
        steps.link(v.tensor_scalar(poly, poly, 1.0 / (2 * n + 1), None, ALU.add))
    steps.link(v.scalar_tensor_tensor(out, z, 2.0, poly, ALU.mult, ALU.mult))


def hybrid(m):
    nc, a, sb, sem = m.nc, m.a, m.sb, m.sem
    scope = ExitStack()
    with scope:
        z = sb("z", [P, NT, HALF], scope=scope)
        bkq = sb("bkq", [P, 2, B_HEADS, SEQ], scope=scope)
        vb, vb_r = m.sb_both("vb", [P, NT, B_HEADS, P], scope=scope)
        beta = sb("beta", [P, NT, B_HEADS], scope=scope)
        g_raw = sb("g_raw", [P, NT, B_HEADS], scope=scope)
        inner = ExitStack()
        with inner:
            qT = sb("qT", [P, 4, SEQ], scope=inner)
            kT = sb("kT", [P, SEQ], scope=inner)
            v_tok = sb("v_tok", [P, NT, P], scope=inner)
            project(m, qT, kT, v_tok, z, bkq, vb, vb_r, beta, g_raw)
            attention(m, qT, kT, v_tok)
        delta_net(m, z, bkq, vb, beta, g_raw)


def project(m, qT, kT, v_tok, z, bkq, vb, vb_r, beta, g_raw):
    nc, a, sb, sem, ps, hT = m.nc, m.a, m.sb, m.sem, m.ps, m.hT
    scope = ExitStack()
    with scope:
        w_vs, w_vs_r = m.sb_both("w_vs", [P, KC, P + 8], scope=scope)
        w_z = sb("w_z", [P, KC, HALF], scope=scope)
        w_ch, w_lo = m.sb_both("w_ch", [P, 2, KC, P], scope=scope)
        x_rest = sb("x_rest", [P, 2, SEQ], F32R, scope=scope)
        conv_w = sb("conv_w", [P, 12, CONV], scope=scope)
        x_hi = ([m.h_r[:, 3 + c, :] for c in range(5)] + [x_rest[:, c, :] for c in range(2)]
                + [w_vs_r[:].rearrange("p c f -> p (c f)")[:, 0:SEQ]])
        x_lo = m.hT_r
        w_hi_first = vb_r[:, 0:4].rearrange("p t i f -> p (t i f)").rearrange("p (j c w) -> p j c w", j=2, w=P)
        w_hi_later = m.h_r[:, 0:2, :].rearrange("p j (c w) -> p j c w", w=P)
        LATER = 9
        w_hi = lambda n: (w_hi_first if n < LATER else w_hi_later)[:, n % 2]
        cos, sin, pos = m.h[:, 0, :], m.h[:, 1, :], m.h[:, 2, :].bitcast(I32)
        raw = sb("raw", [P, 2, CONV - 1 + SEQ], scope=scope)
        small = sb("small", [P, NT, 8], scope=scope)
        eps = sb("eps", [P, 1], scope=scope)
        soft = sb("soft", [P, 6, NT * B_HEADS], scope=scope)
        acc = w_z[:, 0:2, :].rearrange("p a b -> p (a b)")
        sq = w_z[:, 2:6, :].rearrange("p (s a) b -> p s (a b)", s=2)
        tmp = w_z[:, 6:8, :].rearrange("p a b -> p (a b)")

        s_in, s_wv, s_wz = sem("const_in"), sem("wv_in"), sem("wz_in")
        s_x = [sem(f"x_in{q}") for q in range(4)]
        s_w = [sem(f"w_ch_in{j}") for j in range(2)]
        proj, evac, post, fin = sem("projected"), sem("evacuated"), sem("posted"), sem("finished")
        conv, silu = sem("convolved"), sem("activated")
        s_dve, s_act, rooted = sem("proj_dve"), sem("proj_act"), sem("proj_rooted")
        x_taken, x_split, w_taken, w_split = (sem(x) for x in ("x_taken", "x_split", "w_taken", "w_split"))
        ang, trig, soft_in, soft_out, zero = sem("angle"), sem("trig"), sem("soft_in"), sem("soft_out"), sem("padded")
        PI = float(np.float32(3.1415925))

        with nc.Block() as block:
            @block.sync
            def _(sp):
                sp.dma_start(w_vs[:], a["w_vs"]).then_inc(s_wv, 16)
                for q in range(4):
                    cols = slice(2 * q * P, 2 * (q + 1) * P)
                    sp.dma_start(hT[:, :, cols], a["xT"][:, :, cols]).then_inc(s_x[q], 16)
                sp.dma_start(m.cst[:], a["cst"]).then_inc(s_in, 16)
                sp.dma_start(m.rows[:], a["rows"].partition_broadcast(P)).then_inc(s_in, 16)
                sp.dma_start(pos, a["positions"].partition_broadcast(P)).then_inc(s_in, 16)
                sp.dma_start(conv_w[:], a["conv_w"]).then_inc(s_in, 16)
                sp.dma_start(w_z[:], a["w_z"]).then_inc(s_wz, 16)
                for n in range(N_CH):
                    if n >= 2:
                        sp.wait_ge(proj, 2 * NT + n - 1)
                    sp.dma_start(w_ch[:, n % 2], a["w_ch"][n]).then_inc(s_w[n % 2], 16)

            @block.tensor
            def _(pe):
                pe.wait_ge(s_wv, 16)
                for g in range(2 * NT):
                    t = g % NT
                    w, n = (w_vs, P + 8) if g < NT else (w_z, HALF)
                    if g < NT and g % 2 == 0:
                        pe.wait_ge(s_x[g // 2], 16)
                    if g == NT:
                        pe.wait_ge(s_wz, 16)
                    if g >= 4:
                        pe.wait_ge(evac, g - 3)
                    for c in range(KC):
                        mm = pe.matmul(ps[:, g % 4, 0:n], hT[:, c, t * P:(t + 1) * P], w[:, c, :],
                                       start=(c == 0), stop=(c == KC - 1))
                    mm.then_inc(proj, 1)

                def main(n):
                    pe.wait_ge(w_split, n + 1)
                    pe.wait_ge(evac, 2 * NT if n < 2 else 2 * NT + n - 1)
                    for c in range(KC):
                        if n == 0:
                            pe.wait_ge(x_split, c + 1)
                        for u in range(2):
                            cols = slice(u * HALF, (u + 1) * HALF)
                            mm = three(pe, ps[:, 2 * (n % 2) + u, :], (w_hi(n)[:, c, :], w_lo[:, n % 2, c, :]),
                                       (x_hi[c][:, cols], x_lo[:, c, cols]), c == 0, c == KC - 1)
                    mm.then_inc(proj, 1)

                def after(n):
                    if n == 0:
                        pe.wait_ge(s_in, 64)
                    if n < N_QK:
                        pe.wait_ge(evac, 2 * NT + n + 1)
                    else:
                        pe.wait_ge(silu, n - N_QK + 1)
                    if n >= 2:
                        pe.wait_ge(fin, n - 1)
                    b = 4 + 2 * (n % 2)
                    if n < 13:
                        lhs = m.c(C_PERM) if n < N_QK else m.c(C_ONES)
                        for u in range(2):
                            rhs = (raw[:, n % 2, CONV - 1 + u * HALF:CONV - 1 + (u + 1) * HALF] if n < N_QK
                                   else sq[:, n % 2, u * HALF:(u + 1) * HALF])
                            mm = pe.matmul(ps[:, b + u, :], lhs, rhs, start=True, stop=True)
                    else:
                        for t in range(NT):
                            mm = pe.transpose(ps[:, b + t // 4, (t % 4) * P:(t % 4 + 1) * P],
                                              sq[:, n % 2, t * P:(t + 1) * P], m.c(C_ID))
                    mm.then_inc(post, 1)

                for n in range(N_CH):
                    main(n)
                    if n:
                        after(n - 1)
                after(N_CH - 1)

            @block.scalar
            def _(act):
                steps = Steps(act, s_act)

                def take_w(n):
                    act.wait_ge(s_w[n % 2], 16 * (n // 2 + 1))
                    if n >= LATER:
                        act.wait_ge(fin, N_QK)
                    act.activation(w_hi(n), w_ch[:, n % 2], ACT.Copy).then_inc(w_taken, 1)

                for g in range(2 * NT):
                    t = g % NT
                    if g == NT:
                        for q in range(4):
                            act.wait_ge(s_x[q], 16)
                        for c in range(KC - 1):
                            act.activation(x_hi[c], hT[:, c, :], ACT.Copy).then_inc(x_taken, 1)
                        act.wait_ge(proj, NT)
                        act.activation(x_hi[KC - 1], hT[:, KC - 1, :], ACT.Copy).then_inc(x_taken, 1)
                        take_w(0)
                        take_w(1)
                    act.wait_ge(proj, g + 1)
                    if g < NT:
                        steps.link(act.activation(v_tok[:, t, :], ps[:, g % 4, 0:P], ACT.Copy))
                        act.activation(small[:, t, :], ps[:, g % 4, P:P + 8], ACT.Copy).then_inc(evac, 1)
                    else:
                        act.activation(z[:, t, :], ps[:, g % 4, :], ACT.Silu).then_inc(evac, 1)
                act.wait_ge(ang, 1)
                act.activation(sin, sin, ACT.Sin).then_inc(trig, 1)
                act.activation(cos, cos, ACT.Sin).then_inc(trig, 1)
                act.wait_ge(evac, NT)
                act.activation(beta[:], small[:, :, 0:4], ACT.Sigmoid).then_inc(soft_out, 1)
                act.wait_ge(soft_in, 1)
                act.activation(soft[:, 1, :], soft[:, 1, :], ACT.Exp, scale=-1.0).then_inc(soft_out, 1)
                act.wait_ge(s_in, 64)
                act.activation(soft[:, 5, 0:4], m.rows[:, R_ALOG:R_ALOG + 4], ACT.Exp).then_inc(soft_out, 1)
                act.wait_ge(zero, 1)

                def root(n):
                    act.wait_ge(post, n + 1)
                    act.wait_ge(fin, n)
                    act.activation(tmp.rearrange("p (u f) -> p u f", u=2), ps[:, 4 + 2 * (n % 2):6 + 2 * (n % 2), :],
                                   ACT.Sqrt, bias=eps[:, 0:1]).then_inc(rooted, 1)

                for n in range(N_CH):
                    act.wait_ge(proj, 2 * NT + n + 1)
                    if n >= N_QK + 2:
                        act.wait_ge(conv, n - 1 - N_QK)
                    elif n >= 2:
                        act.wait_ge(fin, n - 1)
                    act.activation(raw[:, n % 2, CONV - 1:].rearrange("p (u f) -> p u f", u=2),
                                   ps[:, 2 * (n % 2):2 * (n % 2) + 2, :], ACT.Copy).then_inc(evac, 1)
                    if N_QK <= n - 1 < 13:
                        root(n - 1)
                    if n + 2 < N_CH:
                        take_w(n + 2)
                    if n >= N_QK:
                        act.wait_ge(conv, n - N_QK + 1)
                        if n < 13:
                            kq, i = (1, n - N_QK) if n < 9 else (0, n - 9)
                            steps.link(act.activation(bkq[:, kq, i, :], acc, ACT.Silu))
                            act.activation(sq[:, n % 2, :], bkq[:, kq, i, :], ACT.Square).then_inc(silu, 1)
                        else:
                            act.activation(sq[:, n % 2, :], acc, ACT.Silu).then_inc(silu, 1)

            @block.vector
            def _(v):
                steps = Steps(v, s_dve)
                steps.link(v.memset(eps[:], NORM_EPS))
                v.memset(raw[:, :, 0:CONV - 1], 0.0).then_inc(zero, 1)
                v.wait_ge(s_in, 64)
                turns, angle = raw[:, 0, CONV - 1:], raw[:, 1, CONV - 1:]
                steps.link(v.tensor_copy(sin, pos))
                steps.link(v.tensor_scalar(angle, sin, m.c(C_INV, 1), None, ALU.mult))
                two_pi = 2.0 * np.pi
                p1 = 6.28125
                p2 = float(np.float32(np.round((two_pi - p1) * 2 ** 20) / 2 ** 20))
                p3 = float(np.float32(two_pi - p1 - p2))
                magic = float(1.5 * 2 ** 23)
                for k, dst in enumerate((sin, cos)):
                    steps.link(v.tensor_scalar(turns, angle, float(np.float32(1.0 / two_pi)), 0.25 * k, ALU.mult, ALU.add))
                    steps.link(v.tensor_scalar(turns, turns, magic, None, ALU.add))
                    steps.link(v.tensor_scalar(turns, turns, magic, None, ALU.subtract))
                    steps.link(v.scalar_tensor_tensor(dst, turns, -p1, angle, ALU.mult, ALU.add))
                    steps.link(v.scalar_tensor_tensor(dst, turns, -p2, dst, ALU.mult, ALU.add))
                    steps.link(v.scalar_tensor_tensor(dst, turns, -p3, dst, ALU.mult, ALU.add))
                    if k:
                        steps.link(v.tensor_scalar(dst, dst, float(np.pi / 2), None, ALU.add))
                    last = v.tensor_scalar(dst, dst, PI, -PI, ALU.min, ALU.max)
                    if k:
                        last.then_inc(ang, 1)
                    else:
                        steps.link(last)
                v.wait_ge(evac, NT)
                x = soft[:, 0, :]
                dt_row = m.rows[:, None, R_DT:R_DT + 4].to_broadcast([P, NT, 4])
                steps.link(v.tensor_tensor(x.rearrange("p (t f) -> p t f", f=4), small[:, :, 4:8], dt_row, ALU.add))
                steps.link(v.tensor_scalar(soft[:, 2, :], x, -1.0, None, ALU.mult))
                v.tensor_tensor(soft[:, 1, :], x, soft[:, 2, :], ALU.max).then_inc(soft_in, 1)

                def split_w(n):
                    v.wait_ge(w_taken, n + 1)
                    take_low(v, w_lo[:, n % 2], w_ch[:, n % 2], w_hi(n)).then_inc(w_split, 1)

                split_w(0)
                split_w(1)
                v.wait_ge(proj, 2 * NT)
                for c in range(KC):
                    v.wait_ge(x_taken, c + 1)
                    take_low(v, x_lo[:, c, :], hT[:, c, :], x_hi[c]).then_inc(x_split, 1)

                v.wait_ge(soft_out, 3)
                log1p_steps(v, steps, soft[:, 1, :], soft[:, 1, :], soft[:, 2, :], soft[:, 3, :], soft[:, 4, :])
                steps.link(v.scalar_tensor_tensor(x, x, 0.0, soft[:, 1, :], ALU.max, ALU.add))
                rate = soft[:, 5:6, 0:4].to_broadcast([P, NT, 4])
                steps.link(v.tensor_tensor(g_raw[:], x.rearrange("p (t f) -> p t f", f=4), rate, ALU.mult))
                steps.link(v.tensor_scalar(g_raw[:], g_raw[:], -1.0, None, ALU.mult))
                v.wait_ge(evac, 2 * NT)
                v.wait_ge(trig, 2)

                def finish_tile(n):
                    v.wait_ge(post, n + 1)
                    both = ps[:, 4 + 2 * (n % 2):6 + 2 * (n % 2), :]
                    halves = lambda x: x.rearrange("p (u f) -> p u f", u=2)
                    if n < N_QK:
                        dst = qT[:, n, :] if n < 4 else kT[:]
                        steps.link(v.tensor_tensor(dst, raw[:, n % 2, CONV - 1:], cos, ALU.mult))
                        steps.link(v.tensor_tensor(halves(tmp), both, halves(sin), ALU.mult))
                        v.tensor_tensor(dst, dst, tmp, ALU.add).then_inc(fin, 1)
                    elif n < 13:
                        kq, i = (1, n - N_QK) if n < 9 else (0, n - 9)
                        v.wait_ge(rooted, n - N_QK + 1)
                        steps.link(v.reciprocal(tmp, tmp))
                        v.scalar_tensor_tensor(bkq[:, kq, i, :], tmp, P ** -0.5 if kq else 1.0, bkq[:, kq, i, :],
                                               ALU.mult, ALU.mult).then_inc(fin, 1)
                    else:
                        i = n - 13
                        v.tensor_tensor(vb[:, :, i, :], both.rearrange("p u (t f) -> p (u t) f", f=P),
                                        beta[:, :, i:i + 1].to_broadcast([P, NT, P]), ALU.mult).then_inc(fin, 1)

                for n in range(N_CH):
                    if n >= N_QK:
                        i = n - N_QK
                        v.wait_ge(evac, 2 * NT + n + 1)
                        if i:
                            v.wait_ge(silu, i)
                        steps.link(v.tensor_scalar(acc, raw[:, n % 2, 0:SEQ], conv_w[:, i, 0:1], None, ALU.mult))
                        for k in range(1, CONV):
                            ins = v.scalar_tensor_tensor(acc, raw[:, n % 2, k:k + SEQ], conv_w[:, i, k:k + 1], acc,
                                                         ALU.mult, ALU.add)
                            if k < CONV - 1:
                                steps.link(ins)
                        ins.then_inc(conv, 1)
                    if n + 2 < N_CH:
                        split_w(n + 2)
                    if n:
                        finish_tile(n - 1)
                finish_tile(N_CH - 1)


def attention(m, qT, kT, v_tok):
    nc, sb, sem, ps, hT = m.nc, m.sb, m.sem, m.ps, m.hT
    scope = ExitStack()
    with scope:
        s = sb("scores", [P, 3, A_HEADS, WIN], scope=scope)
        pT = sb("pT", [P, A_HEADS, 2, P], scope=scope)
        ya = sb("ya", [P, 2, HALF], scope=scope)
        mx = sb("mx", [P, 3, 4, A_HEADS], scope=scope)
        scored, masked, expd = sem("scored"), sem("masked"), sem("exponentiated")
        turned, p_out, mixed, y_out, y_turned, y_done = (sem(x) for x in
            ("p_turned", "p_out", "pv_done", "ya_out", "ya_turned", "ya_done"))
        s_dve, s_sum = sem("att_dve"), sem("denominators")
        maxed, expsink = sem("maxed"), sem("expsink")
        s_h = sem("h_in")

        with nc.Block() as block:
            @block.sync
            def _(sp):
                sp.dma_start(m.h[:], m.a["x"].rearrange("(t p) d -> p t d", p=P)).then_inc(s_h, 16)
                sp.wait_ge(s_h, 16)

            @block.tensor
            def _(pe):
                def scores(t, q):
                    if t and q == 0:
                        pe.wait_ge(masked, t)
                    lo = 0 if t else P
                    for hd in range(4 * q, 4 * q + 4):
                        b, i = 64 * (hd // 4), hd % 4
                        mm = pe.matmul(ps[:, hd // 2, (hd % 2) * WIN + lo:(hd % 2 + 1) * WIN],
                                       qT[b:b + 64, i, t * P:(t + 1) * P],
                                       kT[b:b + 64, (t - 1) * P + lo:(t + 1) * P], start=True, stop=True)
                    if q:
                        mm.then_inc(scored, 1)

                def turn_p(t, q):
                    if q == 0:
                        pe.wait_ge(expd, t + 1)
                    if 2 * t + q:
                        pe.wait_ge(p_out, 2 * t + q)
                    for hd in range(4 * q, 4 * q + 4):
                        for k in range(0 if t else 1, 2):
                            at = (hd - 4 * q) * 2 + k
                            mm = pe.transpose(ps[:, 4 + at // 4, (at % 4) * P:(at % 4 + 1) * P],
                                              s[:, t % 3, hd, k * P:(k + 1) * P], m.c(C_ID))
                    mm.then_inc(turned, 1)

                def values(t):
                    pe.wait_ge(p_out, 2 * t + 2)
                    if t:
                        pe.wait_ge(y_out, t)
                    for hd in range(A_HEADS):
                        b = 64 * (hd // 4)
                        for k in range(0 if t else 1, 2):
                            mm = pe.matmul(ps[:, 6, hd * 64:(hd + 1) * 64], pT[:, hd, k, :],
                                           v_tok[:, t - 1 + k, b:b + 64], start=(k == (0 if t else 1)), stop=(k == 1))
                    mm.then_inc(mixed, 1)

                def turn_y(t):
                    pe.wait_ge(y_out, t + 1)
                    if t:
                        pe.wait_ge(y_done, t)
                    for c in range(4):
                        mm = pe.transpose(ps[:, 7, c * P:(c + 1) * P], ya[:, t % 2, c * P:(c + 1) * P], m.c(C_ID))
                    mm.then_inc(y_turned, 1)

                for t in range(NT + 3):
                    for q in range(2):
                        if 2 <= t < NT + 2:
                            turn_p(t - 2, q)
                        if t < NT:
                            scores(t, q)
                    if t >= 3:
                        turn_y(t - 3)
                    if 2 <= t < NT + 2:
                        values(t - 2)

            @block.vector
            def _(v):
                steps = Steps(v, s_dve)

                def softmax_in(t):
                    v.wait_ge(scored, t + 1)
                    if t >= 3:
                        v.wait_ge(turned, 2 * t - 4)
                    lo = 0 if t else P
                    n = WIN - lo
                    sc = s[:, t % 3, :, lo:]
                    raw = ps[:, 0:4, :].rearrange("p b (h w) -> p (b h) w", w=WIN)[:, :, lo:]
                    mask = m.cst[:, None, C_AMASK + lo:C_AMASK + WIN].to_broadcast([P, A_HEADS, n])
                    ins = v.scalar_tensor_tensor(sc, raw, A_HD ** -0.5, mask, ALU.mult, ALU.add)
                    ins.then_inc(masked, 1)
                    v.wait_ge(masked, t + 1)
                    mt = mx[:, t % 3]
                    steps.link(v.tensor_reduce(mt[:, 0, :], sc, AX, ALU.max))
                    steps.link(v.tensor_tensor(mt[:, 0, :], mt[:, 0, :], m.rows[:, R_SINK:R_SINK + 8], ALU.max))
                    steps.link(v.tensor_tensor(mt[:, 1, :], m.rows[:, R_SINK:R_SINK + 8], mt[:, 0, :], ALU.subtract))
                    v.tensor_scalar(mt[:, 0, :], mt[:, 0, :], -1.0, None, ALU.mult).then_inc(maxed, 1)

                def normalise(t):
                    mt = mx[:, t % 3]
                    v.wait_ge(expd, t + 1)
                    steps.link(v.tensor_tensor(mt[:, 2, :], mt[:, 2, :], mt[:, 1, :], ALU.add))
                    steps.link(v.reciprocal(mt[:, 3, :], mt[:, 2, :]))
                    v.wait_ge(mixed, t + 1)
                    if t >= 2:
                        v.wait_ge(y_turned, t - 1)
                    v.tensor_tensor(ya[:, t % 2, :].rearrange("p (h d) -> p h d", d=64),
                                    ps[:, 6, :].rearrange("p (h d) -> p h d", d=64),
                                    mt[:, 3, :, None].to_broadcast([P, A_HEADS, 64]), ALU.mult).then_inc(y_out, 1)

                for t in range(NT + 2):
                    if t < NT:
                        softmax_in(t)
                    if t >= 2:
                        normalise(t - 2)

            @block.scalar
            def _(act):
                def exps(t):
                    act.wait_ge(maxed, t + 1)
                    lo = 0 if t else P
                    mt = mx[:, t % 3]
                    act.activation(mt[:, 1, :], mt[:, 1, :], ACT.Exp).then_inc(expsink, 1)
                    for hd in range(A_HEADS):
                        ins = act.activation(s[:, t % 3, hd, lo:], s[:, t % 3, hd, lo:], ACT.Exp,
                                             bias=mt[:, 0, hd:hd + 1], accum_out=mt[:, 2, hd:hd + 1])
                    act.wait_ge(expsink, t + 1)
                    ins.then_inc(expd, 1)

                def copies(t):
                    for q in range(2):
                        act.wait_ge(turned, 2 * t + q + 1)
                        if q == 0 and t:
                            act.wait_ge(mixed, t)
                        lo = 0 if t else 1
                        act.activation(pT[:, 4 * q:4 * q + 4, lo:, :],
                                       ps[:, 4:6, :].rearrange("p b (h k w) -> p (b h) k w", k=2, w=P)[:, :, lo:, :],
                                       ACT.Copy).then_inc(p_out, 1)

                def y_copy(t):
                    act.wait_ge(y_turned, t + 1)
                    act.activation(hT[:, 0:4, t * P:(t + 1) * P], ps[:, 7, :].rearrange("p (c w) -> p c w", w=P),
                                   ACT.Copy).then_inc(y_done, 1)

                for t in range(NT + 3):
                    if 2 <= t < NT + 2:
                        copies(t - 2)
                    if t < NT:
                        exps(t)
                    if t >= 3:
                        y_copy(t - 3)


def delta_net(m, z, bkq, vb, beta, g_raw):
    nc, sb, sem, ps, hT = m.nc, m.sb, m.sem, m.ps, m.hT
    scope = ExitStack()
    H, L = B_HEADS, LEVELS
    with scope:
        def tile(name, k=2):
            return sb(name, [P, k, H, P], scope=scope)

        diag, decay, expg = tile("diag"), tile("decay"), tile("expg")
        AT, attnT, kbg, kg, qg = tile("AT"), tile("attnT"), tile("kbg"), tile("kg"), tile("qg")
        CT, X, T, TT = tile("CT"), tile("X"), tile("T"), tile("TT")
        state = tile("state", 1)[:, 0]
        wT, u, v_new, o = CT, X, T, AT
        junk = diag
        Gc = sb("Gc", [P, NT, H], scope=scope)
        bg = sb("bg", [P, NT, H], scope=scope)
        kgs = sb("kgs", [P, 2, H], scope=scope)
        ms = sb("ms", [P, 2, H], scope=scope)
        eps = sb("dn_eps", [P, 1], scope=scope)

        bank = lambda b: ps[:, b, :].rearrange("p (h w) -> p h w", w=P)
        col = lambda x: x[:, :, None].to_broadcast([P, H, P])
        mat = lambda at: m.cst[:, None, at:at + P].to_broadcast([P, H, P])
        span = lambda t: slice(t * P, (t + 1) * P)

        summed, gc_out, bg_exp, s_dve, s_act = (sem(f"dn_{x}") for x in ("summed", "gc", "bg_exp", "dve", "act"))
        diagd, gb, diff, expd, masked, qg_out = (sem(f"dn_{x}") for x in ("diag", "gb", "diff", "exp", "mask", "qg"))
        kk, k_turned, at_out, keys_out = (sem(f"dn_{x}") for x in ("kk", "k_turned", "at", "keys"))
        ct_out, x_mm, x_out, tx_mm, t_out = (sem(f"dn_{x}") for x in ("ct", "x_mm", "x_out", "tx_mm", "t_out"))
        uw_mm, uw_out, p1_mm, v_out, o_mm, s_out = (sem(f"dn_{x}") for x in
            ("uw_mm", "uw_out", "p1", "v_new", "o_mm", "state"))
        squared, rms_out = sem("dn_squared"), sem("dn_rms")
        y_out, y_turned, y_done = (sem(f"dn_{x}") for x in ("y", "y_turned", "y_done"))

        lv = lambda t, l: (t // 2) * 2 * L + 2 * l + t % 2 + 1

        with nc.Block() as block:
            @block.tensor
            def _(pe):
                pe.matmul(ps[:, 0, 0:NT * H], m.c(C_UTRI), g_raw[:].rearrange("p t h -> p (t h)"),
                          start=True, stop=True).then_inc(summed, 1)
                for pair in range(NT // 2):
                    ts = (2 * pair, 2 * pair + 1)
                    for t in ts:
                        j = t % 2
                        pe.wait_ge(diagd, t + 1)
                        if t >= 2:
                            pe.wait_ge(y_done, t - 1)
                        pe.matmul(ps[:, 4 * j, :], m.c(C_ONES), diag[:, j].rearrange("p h w -> p (h w)"),
                                  start=True, stop=True).then_inc(gb, 1)
                    for t in ts:
                        j = t % 2
                        if t >= 2:
                            pe.wait_ge(y_out, t - 1)
                            pe.wait_ge(s_out, t)
                        for hd in range(H):
                            mm = pe.matmul(ps[:, 4 * j + 1 + hd // 2, (hd % 2) * 2 * P:(hd % 2 + 1) * 2 * P]
                                           .rearrange("p (a w) -> p a w", a=2),
                                           bkq[:, 0, hd, span(t)], bkq[:, :, hd, span(t)], start=True, stop=True)
                        mm.then_inc(kk, 1)
                        for hd in range(H):
                            mm = pe.transpose(ps[:, 4 * j + 3, hd * P:(hd + 1) * P], bkq[:, 0, hd, span(t)], m.c(C_ID))
                        mm.then_inc(k_turned, 1)
                    for l in range(L):
                        for t in ts:
                            j = t % 2
                            pe.wait_ge(ct_out, lv(t, l))
                            if l:
                                pe.wait_ge(t_out, lv(t, l - 1))
                            else:
                                pe.wait_ge(expd, t + 1)
                            for hd in range(H):
                                o_ = ps[:, 4 * j, hd * P:(hd + 1) * P]
                                if l:
                                    mm = pe.matmul(o_, CT[:, j, hd], T[:, j, hd], start=True, stop=True)
                                else:
                                    mm = pe.transpose(o_, CT[:, j, hd], m.c(C_ID))
                            mm.then_inc(x_mm, 1)
                        for t in ts:
                            j = t % 2
                            pe.wait_ge(x_out, lv(t, l))
                            for hd in range(H):
                                w = slice(hd * P, (hd + 1) * P)
                                if l == 0:
                                    mm = pe.transpose(ps[:, 4 * j + 2, w], X[:, j, hd], m.c(C_ID))
                                else:
                                    if l < L - 1:
                                        pe.matmul(ps[:, 4 * j + 1, w], TT[:, j, hd], X[:, j, hd], start=True, stop=True)
                                    mm = pe.matmul(ps[:, 4 * j + 2, w], X[:, j, hd], TT[:, j, hd], start=True, stop=True)
                            mm.then_inc(tx_mm, 1)
                    for t in ts:
                        j = t % 2
                        pe.wait_ge(t_out, lv(t, L - 1))
                        pe.wait_ge(keys_out, t + 1)
                        for hd in range(H):
                            pe.matmul(ps[:, 4 * j + 3, hd * P:(hd + 1) * P], TT[:, j, hd], vb[:, t, hd],
                                      start=True, stop=True)
                            mm = pe.matmul(ps[:, 4 * j, hd * P:(hd + 1) * P], kbg[:, j, hd], TT[:, j, hd],
                                           start=True, stop=True)
                        mm.then_inc(uw_mm, 1)
                    for t in ts:
                        j = t % 2
                        pe.wait_ge(uw_out, t + 1)
                        pe.wait_ge(s_out, t + 1)
                        for hd in range(H):
                            mm = pe.matmul(ps[:, 4 * j + 1, hd * P:(hd + 1) * P], wT[:, j, hd], state[:, hd],
                                           start=True, stop=True)
                        mm.then_inc(p1_mm, 1)
                        pe.wait_ge(v_out, t + 1)
                        pe.wait_ge(qg_out, t + 1)
                        for hd in range(H):
                            w = slice(hd * P, (hd + 1) * P)
                            pe.matmul(ps[:, 4 * j + 3, w], kg[:, j, hd], v_new[:, j, hd], start=True, stop=True)
                            pe.matmul(ps[:, 4 * j + 2, w], qg[:, j, hd], state[:, hd], start=True, stop=False)
                            mm = pe.matmul(ps[:, 4 * j + 2, w], attnT[:, j, hd], v_new[:, j, hd], start=False, stop=True)
                        mm.then_inc(o_mm, 1)
                    for t in ts:
                        j = t % 2
                        pe.wait_ge(y_out, t + 1)
                        for hd in range(H):
                            mm = pe.transpose(ps[:, 4 * j, hd * P:(hd + 1) * P], o[:, j, hd], m.c(C_ID))
                        mm.then_inc(y_turned, 1)

            @block.vector
            def _(v):
                steps = Steps(v, s_dve)
                steps.link(v.memset(eps[:], NORM_EPS))
                v.memset(state, 0.0).then_inc(s_out, 1)
                v.wait_ge(summed, 1)
                v.tensor_copy(Gc[:].rearrange("p t h -> p (t h)"), ps[:, 0, 0:NT * H]).then_inc(gc_out, 1)
                v.wait_ge(bg_exp, 1)
                v.wait_ge(gc_out, 1)
                steps.link(v.tensor_tensor(bg[:], bg[:], beta[:], ALU.mult))
                for pair in range(NT // 2):
                    ts = (2 * pair, 2 * pair + 1)
                    for t in ts:
                        v.tensor_tensor(diag[:, t % 2], mat(C_ID), col(Gc[:, t]), ALU.mult).then_inc(diagd, 1)
                    for t in ts:
                        j = t % 2
                        v.wait_ge(gb, t + 1)
                        g = bank(4 * j)
                        steps.link(v.tensor_tensor(decay[:, j], g, col(Gc[:, t]), ALU.subtract))
                        v.tensor_tensor(kgs[:, j], g[:, :, P - 1], Gc[:, t], ALU.subtract)
                        v.tensor_scalar(decay[:, j], decay[:, j], 0.0, None, ALU.min).then_inc(diff, 1)
                    for t in ts:
                        j = t % 2
                        v.wait_ge(kk, t + 1)
                        v.wait_ge(masked, t + 1)
                        both = ps[:, 4 * j + 1:4 * j + 3, :].rearrange("p b (h a w) -> p (b h) a w", a=2, w=P)
                        v.tensor_tensor(AT[:, j], both[:, :, 0, :], decay[:, j], ALU.mult).then_inc(at_out, 1)
                        steps.link(v.tensor_tensor(attnT[:, j], both[:, :, 1, :], decay[:, j], ALU.mult))
                        v.wait_ge(k_turned, t + 1)
                        steps.link(v.tensor_tensor(kbg[:, j], bank(4 * j + 3), col(bg[:, t]), ALU.mult))
                        v.tensor_tensor(kg[:, j], bank(4 * j + 3), col(kgs[:, j]), ALU.mult).then_inc(keys_out, 1)
                    for l in range(L):
                        for t in ts:
                            j = t % 2
                            v.wait_ge(x_mm, lv(t, l))
                            v.tensor_tensor(X[:, j], bank(4 * j), col(beta[:, t]), ALU.mult).then_inc(x_out, 1)
                        for t in ts:
                            j = t % 2
                            v.wait_ge(tx_mm, lv(t, l))
                            if l == 0:
                                v.wait_ge(x_out, lv(t, l))
                                steps.link(v.tensor_tensor(T[:, j], mat(C_ID), X[:, j], ALU.subtract))
                                ins = v.tensor_tensor(TT[:, j], mat(C_ID), bank(4 * j + 2), ALU.subtract)
                            else:
                                if l < L - 1:
                                    steps.link(v.tensor_tensor(T[:, j], T[:, j], bank(4 * j + 1), ALU.subtract))
                                ins = v.tensor_tensor(TT[:, j], TT[:, j], bank(4 * j + 2), ALU.subtract)
                            ins.then_inc(t_out, 1)
                    for t in ts:
                        j = t % 2
                        v.wait_ge(p1_mm, t + 1)
                        v.tensor_tensor(v_new[:, j], u[:, j], bank(4 * j + 1), ALU.subtract).then_inc(v_out, 1)
                        v.wait_ge(o_mm, t + 1)
                        for hd in range(H):
                            ins = v.scalar_tensor_tensor(state[:, hd], state[:, hd], expg[:, j, hd, P - 1:P],
                                                         ps[:, 4 * j + 3, hd * P:(hd + 1) * P], ALU.mult, ALU.add)
                        ins.then_inc(s_out, 1)
                    for t in ts:
                        j = t % 2
                        v.wait_ge(rms_out, t + 1)
                        steps.link(v.reciprocal(ms[:, j], ms[:, j]))
                        steps.link(v.tensor_tensor(o[:, j], bank(4 * j + 2), col(ms[:, j]), ALU.mult))
                        norm_g = m.rows[:, None, R_NORM:R_NORM + P].to_broadcast([P, H, P])
                        steps.link(v.tensor_tensor(o[:, j], o[:, j], norm_g, ALU.mult))
                        v.tensor_tensor(o[:, j], o[:, j], z[:, t, :].rearrange("p (h w) -> p h w", w=P),
                                        ALU.mult).then_inc(y_out, 1)

            @block.scalar
            def _(act):
                steps = Steps(act, s_act)
                act.wait_ge(gc_out, 1)
                act.activation(bg[:], Gc[:], ACT.Exp).then_inc(bg_exp, 1)
                for pair in range(NT // 2):
                    ts = (2 * pair, 2 * pair + 1)
                    for t in ts:
                        j = t % 2
                        act.wait_ge(diff, t + 1)
                        act.activation(expg[:, j], bank(4 * j), ACT.Exp)
                        act.activation(kgs[:, j], kgs[:, j], ACT.Exp)
                        act.activation(decay[:, j], decay[:, j], ACT.Exp).then_inc(expd, 1)
                    for t in ts:
                        j = t % 2
                        act.wait_ge(uw_mm, t + 1)
                        act.activation(u[:, j], bank(4 * j + 3), ACT.Copy)
                        act.activation(wT[:, j], bank(4 * j), ACT.Copy).then_inc(uw_out, 1)
                    for t in ts:
                        j = t % 2
                        act.wait_ge(o_mm, t + 1)
                        for hd in range(H):
                            ins = act.activation(junk[:, j, hd], ps[:, 4 * j + 2, hd * P:(hd + 1) * P], ACT.Square,
                                                 accum_out=ms[:, j, hd:hd + 1])
                        ins.then_inc(squared, 1)
                    for t in ts:
                        j = t % 2
                        act.wait_ge(squared, t + 1)
                        act.activation(ms[:, j], ms[:, j], ACT.Sqrt, scale=1.0 / P, bias=eps[:, 0:1]).then_inc(rms_out, 1)
                    for t in ts:
                        act.wait_ge(y_turned, t + 1)
                        act.activation(hT[:, 4:8, span(t)], bank(4 * (t % 2)), ACT.Copy).then_inc(y_done, 1)

            @block.gpsimd
            def _(pool):
                for pair in range(NT // 2):
                    ts = (2 * pair, 2 * pair + 1)
                    for t in ts:
                        j = t % 2
                        pool.wait_ge(expd, t + 1)
                        pool.tensor_tensor(decay[:, j], decay[:, j], mat(C_UTRI), ALU.mult).then_inc(masked, 1)
                    for l in range(L):
                        for t in ts:
                            j = t % 2
                            pool.wait_ge(at_out, t + 1)
                            if l:
                                pool.wait_ge(x_mm, lv(t, l - 1))
                            pool.tensor_tensor(CT[:, j], AT[:, j], mat(C_LEVEL + l * P), ALU.mult).then_inc(ct_out, 1)
                        if l == 0:
                            for t in ts:
                                j = t % 2
                                pool.tensor_tensor(qg[:, j], bkq[:, 1, :, span(t)], expg[:, j], ALU.mult).then_inc(qg_out, 1)


def recurrent(m):
    nc, a, sb, sem, ps, hT = m.nc, m.a, m.sb, m.sem, m.ps, m.hT
    scope = ExitStack()
    with scope:
        w_ch, w_lo = m.sb_both("rw_ch", [P, 2, KC, P], scope=scope)
        w_hi_place, w_hi = m.sb_both("rw_hi", [P, 2, KC, P], scope=scope)
        gates, x_hi = m.sb_both("rx_hi", [P, KC, SEQ], scope=scope)
        r, i = gates[:, 0:4, :], gates[:, 4:8, :]
        root = [w[:, k].rearrange("p c w -> p (c w)") for w in (w_ch, w_hi_place) for k in range(2)]
        x_lo = m.hT_r
        w_ax = sb("w_ax", [P, 2, 4, 2, 2 * P], scope=scope)
        vec = sb("rec_vec", [P, 8, KC], scope=scope)
        rate = sb("rate", [P, 6, KC], scope=scope)
        gate = sb("gelu", [P, KC, SEQ], scope=scope)
        xr = sb("xr", [P, KC, SEQ], scope=scope)
        raw = gate[:, 5:KC, :].rearrange("p c s -> p (c s)")[:, 0:2 * (CONV - 1 + SEQ)].rearrange("p (j s) -> p j s", j=2)
        s_vec, s_ax, s_w = sem("vec_in"), sem("ax_in"), [sem(f"rw_in{j}") for j in range(2)]
        proj, evac, conv, zero = sem("r_proj"), sem("r_evac"), sem("r_conv"), sem("r_zero")
        s_dve, ax_mm, ax_out, decays, scanned = sem("r_dve"), sem("ax_mm"), sem("ax_out"), sem("r_decays"), sem("scanned")
        x_taken, x_split, w_taken, w_split = (sem(x) for x in ("rx_taken", "rx_split", "rw_taken", "rw_split"))
        lam_in, lam_exp, rate_out, rooted, prepared = (sem(x) for x in ("lam_in", "lam_exp", "rate_out", "rooted", "prepared"))
        driven = sem("r_driven")
        N = 2 * KC

        with nc.Block() as block:
            @block.gpsimd
            def _(pool):
                for c in range(KC):
                    pool.wait_ge(decays, c - c % 2 + 2)
                    pool.tensor_tensor(i[:, c % 4, :], i[:, c % 4, :], xr[:, c, :], ALU.mult).then_inc(driven, 1)

            @block.sync
            def _(sp):
                sp.dma_start(vec[:], a["rec_vec"]).then_inc(s_vec, 16)
                for n in range(N):
                    if n >= 2:
                        sp.wait_ge(proj, n - 1)
                    sp.dma_start(w_ch[:, n % 2], a["rec_w_ch"][n]).then_inc(s_w[n % 2], 16)
                    if n == 3:
                        sp.dma_start(w_ax[:], a["w_ax"]).then_inc(s_ax, 16)

            @block.tensor
            def _(pe):
                for n in range(N):
                    j = n % 2
                    pe.wait_ge(w_split, n + 1)
                    if n >= 2:
                        pe.wait_ge(evac, n - 1)
                    for c in range(KC):
                        if n == 0:
                            pe.wait_ge(x_split, c + 1)
                        for hf in range(2):
                            cols = slice(hf * HALF, (hf + 1) * HALF)
                            mm = three(pe, ps[:, 2 * j + hf, :], (w_hi[:, j, c, :], w_lo[:, j, c, :]),
                                       (x_hi[:, c, cols], x_lo[:, c, cols]), c == 0, c == KC - 1)
                    mm.then_inc(proj, 1)
                pe.wait_ge(s_ax, 16)
                for c in range(KC):
                    hd, q = c // 2, c % 2
                    pe.wait_ge(conv, KC)
                    if c == 1:
                        pe.wait_ge(evac, N)
                    for x in range(2):
                        k = 2 * c + x
                        if k >= 4:
                            pe.wait_ge(ax_out, k - 3)
                        for hf in range(2):
                            for kt in range(2):
                                mm = pe.matmul(ps[:, 4 - 4 * q + 2 * x + hf, :], w_ax[:, x, hd, kt, q * P:(q + 1) * P],
                                               xr[:, 2 * hd + kt, hf * HALF:(hf + 1) * HALF], start=(kt == 0), stop=(kt == 1))
                        mm.then_inc(ax_mm, 1)

            @block.scalar
            def _(act):
                def take_w(n):
                    act.wait_ge(s_w[n % 2], 16 * (n // 2 + 1))
                    act.activation(w_hi[:, n % 2], w_ch[:, n % 2], ACT.Copy).then_inc(w_taken, 1)

                take_w(0)
                for c in range(KC):
                    act.activation(x_hi[:, c, :], hT[:, c, :], ACT.Copy).then_inc(x_taken, 1)
                take_w(1)
                act.wait_ge(lam_in, 1)
                act.activation(rate[:, 1, :], rate[:, 1, :], ACT.Exp, scale=-1.0).then_inc(lam_exp, 1)
                act.wait_ge(zero, 1)
                for n in range(N):
                    act.wait_ge(proj, n + 1)
                    src = ps[:, 2 * (n % 2):2 * (n % 2) + 2, :]
                    if n < KC:
                        if n >= 2:
                            act.wait_ge(conv, n - 1)
                        act.activation(raw[:, n % 2, CONV - 1:].rearrange("p (u f) -> p u f", u=2), src,
                                       ACT.Copy).then_inc(evac, 1)
                    else:
                        if n == KC + 5:
                            act.wait_ge(conv, KC)
                        act.activation(gate[:, n - KC, :].rearrange("p (u f) -> p u f", u=2), src,
                                       ACT.Gelu_apprx_tanh).then_inc(evac, 1)
                    if n + 2 < N:
                        take_w(n + 2)
                act.wait_ge(rate_out, 1)

                def decays_of(c):
                    j, b = c % 4, 4 - 4 * (c % 2)
                    for x, dst in enumerate((r, i)):
                        act.wait_ge(ax_mm, 2 * c + x + 1)
                        if c >= 4:
                            act.wait_ge(scanned, c - 3)
                        act.activation(dst[:, j, :].rearrange("p (u f) -> p u f", u=2), ps[:, b + 2 * x:b + 2 * x + 2, :],
                                       ACT.Sigmoid, bias=vec[:, 5 + x, c:c + 1]).then_inc(ax_out, 1)
                    act.wait_ge(ax_out, 2 * c + 2)
                    act.activation(root[j], r[:, j, :], ACT.Tanh, scale=rate[:, 0, c:c + 1])
                    act.activation(r[:, j, :], r[:, j, :], ACT.Exp, scale=rate[:, 5, c:c + 1]).then_inc(decays, 1)

                for c in range(2):
                    decays_of(c)
                for c0 in range(0, KC, 2):
                    for c in range(c0 + 2, min(c0 + 4, KC)):
                        decays_of(c)
                    for d in (c0, c0 + 1):
                        act.wait_ge(prepared, d + 1)
                        act.activation(root[d % 4], root[d % 4], ACT.Sqrt).then_inc(rooted, 1)

            @block.vector
            def _(v):
                steps = Steps(v, s_dve)
                v.memset(raw[:, :, 0:CONV - 1], 0.0).then_inc(zero, 1)

                def split_w(n):
                    v.wait_ge(w_taken, n + 1)
                    take_low(v, w_lo[:, n % 2], w_ch[:, n % 2], w_hi[:, n % 2]).then_inc(w_split, 1)

                split_w(0)
                for c in range(KC):
                    v.wait_ge(x_taken, c + 1)
                    take_low(v, x_lo[:, c, :], hT[:, c, :], x_hi[:, c, :]).then_inc(x_split, 1)
                split_w(1)
                v.wait_ge(s_vec, 16)
                lam = vec[:, 7, :]
                steps.link(v.tensor_scalar(rate[:, 0, :], lam, -1.0, None, ALU.mult))
                v.tensor_tensor(rate[:, 1, :], lam, rate[:, 0, :], ALU.max).then_inc(lam_in, 1)
                v.wait_ge(lam_exp, 1)
                log1p_steps(v, steps, rate[:, 1, :], rate[:, 1, :], rate[:, 2, :], rate[:, 3, :], rate[:, 4, :])
                steps.link(v.scalar_tensor_tensor(rate[:, 0, :], rate[:, 0, :], 0.0, rate[:, 1, :], ALU.max, ALU.add))
                steps.link(v.tensor_scalar(rate[:, 0, :], rate[:, 0, :], 8.0, None, ALU.mult))
                v.tensor_scalar(rate[:, 5, :], rate[:, 0, :], -1.0, None, ALU.mult).then_inc(rate_out, 1)
                for n in range(KC):
                    v.wait_ge(evac, n + 1)
                    dst = xr[:, n, :]
                    steps.link(v.tensor_scalar(dst, raw[:, n % 2, 0:SEQ], vec[:, 0, n:n + 1], vec[:, 4, n:n + 1],
                                               ALU.mult, ALU.add))
                    for k in range(1, CONV):
                        ins = v.scalar_tensor_tensor(dst, raw[:, n % 2, k:k + SEQ], vec[:, k, n:n + 1], dst,
                                                     ALU.mult, ALU.add)
                        if k < CONV - 1:
                            steps.link(ins)
                    ins.then_inc(conv, 1)
                    split_w(n + 2)
                for n in range(KC, N - 2):
                    split_w(n + 2)
                v.wait_ge(conv, KC)
                for c0 in range(0, KC, 2):
                    for c in (c0, c0 + 1):
                        s, den = root[c % 4], xr[:, c, :]
                        v.wait_ge(driven, c + 1)
                        steps.link(v.tensor_scalar(den, s, 1.0, None, ALU.add))
                        steps.link(v.reciprocal(den, den))
                        v.scalar_tensor_tensor(s, s, 2.0, den, ALU.mult, ALU.mult).then_inc(prepared, 1)
                    for c in (c0, c0 + 1):
                        s, hc, j = root[c % 4], xr[:, c, :], c % 4
                        v.wait_ge(rooted, c + 1)
                        steps.link(v.tensor_tensor(i[:, j, :], i[:, j, :], s, ALU.mult))
                        steps.link(v.tensor_tensor_scan(hc, r[:, j, :], i[:, j, :], 0.0, ALU.mult, ALU.add))
                        v.tensor_tensor(hT[:, c, :], gate[:, c, :], hc, ALU.mult).then_inc(scanned, 1)


def three(pe, out, lhs, rhs, start, stop):
    pe.matmul(out, lhs[0], rhs[0], start=start, stop=False)
    pe.matmul(out, lhs[0], rhs[1], start=False, stop=False)
    return pe.matmul(out, lhs[1], rhs[0], start=False, stop=stop)


def take_low(v, low, whole, high):
    return v.tensor_tensor(low, whole, high.bitcast(F32), ALU.subtract)


class LayerNorm:

    def __init__(self, m, name, scope, g_row, b_row):
        self.h, self.g_row, self.b_row = m.h, g_row, b_row
        self.stats = m.sb(f"{name}_stats", [P, 2, 17], scope=scope)
        self.eps = m.sb(f"{name}_eps", [P, 1], scope=scope)
        self.varied, self.rooted, self.scaled, self.normed, self.gained, self.ready = (
            m.sem(f"{name}_{x}") for x in ("varied", "rooted", "scaled", "normed", "gained", "ready"))

    def statistics(self, v, steps, t):
        x, st = self.h[:, t, :], self.stats[:, t % 2]
        v.bn_stats(st[:, 0:6], x[:, 0:HALF])
        steps.link(v.bn_stats(st[:, 6:12], x[:, HALF:]))
        v.bn_aggr(st[:, 12:14], st[:, 0:12]).then_inc(self.varied, 1)

    def root(self, act, t):
        st = self.stats[:, t % 2]
        act.wait_ge(self.varied, t + 1)
        act.activation(st[:, 14:15], st[:, 13:14], ACT.Sqrt, bias=self.eps[:, 0:1]).then_inc(self.rooted, 1)

    def scale(self, v, steps, t):
        st = self.stats[:, t % 2]
        v.wait_ge(self.rooted, t + 1)
        steps.link(v.reciprocal(st[:, 15:16], st[:, 14:15]))
        v.scalar_tensor_tensor(st[:, 16:17], st[:, 12:13], -1.0, st[:, 15:16], ALU.mult, ALU.mult).then_inc(self.scaled, 1)

    def normalise(self, act, t):
        x, st = self.h[:, t, :], self.stats[:, t % 2]
        act.wait_ge(self.scaled, t + 1)
        act.activation(x, x, ACT.Identity, scale=st[:, 15:16], bias=st[:, 16:17]).then_inc(self.normed, 1)

    def gain(self, v, t):
        v.wait_ge(self.normed, t + 1)
        v.tensor_tensor(self.h[:, t, :], self.h[:, t, :], self.g_row, ALU.mult).then_inc(self.gained, 1)

    def shift(self, pool, t):
        pool.wait_ge(self.gained, t + 1)
        pool.tensor_tensor(self.h[:, t, :], self.h[:, t, :], self.b_row, ALU.add).then_inc(self.ready, 1)


def out_projection(m, layer, raw, landed):
    nc, a, sb, sem, ps, h, hT = m.nc, m.a, m.sb, m.sem, m.ps, m.h, m.hT
    scope = ExitStack()
    n_ = lambda x: f"{x}_o{layer}"
    with scope:
        w_out, w_lo = m.sb_both(n_("w_out"), [P, KC, D], scope=scope)
        w_hi = sb(n_("w_out_hi"), [P, KC, D], F32R, scope=scope)
        y_hi = sb(n_("y_hi"), [P, KC, SEQ], F32R, scope=scope)
        y_lo = m.hT_r
        ln = sb(n_("ln"), [P, 2, D], scope=scope)
        norm = LayerNorm(m, n_("norm"), scope, ln[:, 0, :], ln[:, 1, :])
        ready = norm.ready
        w_route = sb(n_("w_route"), [P, KC, ROUTES], scope=scope)
        s_wr = sem(n_("w_route_in"))
        s_w = [sem(n_(f"w_in{q}")) for q in range(4)]
        s_ln, proj, summed, turned, out, stored, s_dve = (sem(n_(x)) for x in
            ("ln_in", "proj", "summed", "turned", "ht_out", "h_stored", "dve"))
        y_taken, y_split, w_taken, w_split = (sem(n_(x)) for x in ("y_taken", "y_split", "w_taken", "w_split"))
        order = [("y", 0), ("y", 1), ("w", 0), ("w", 1), ("y", 2), ("w", 2), ("w", 3), ("y", 3),
                 ("w", 4), ("w", 5), ("y", 4), ("w", 6), ("w", 7), ("y", 5), ("y", 6), ("y", 7)]
        with nc.Block() as block:
            @block.gpsimd
            def _(pool):
                pool.wait_ge(s_ln, 16)
                for t in range(NT):
                    norm.shift(pool, t)

            @block.sync
            def _(sp):
                for q in range(4):
                    sp.dma_start(w_out[:, 2 * q:2 * q + 2, :], a["w_out"][layer][:, 2 * q:2 * q + 2, :]).then_inc(s_w[q], 16)
                sp.dma_start(ln[:], a["ln"][layer, 0].partition_broadcast(P)).then_inc(s_ln, 16)
                sp.dma_start(w_route[:], a["w_route"][layer]).then_inc(s_wr, 16)
                for k in range(RING - 1):
                    load_piece(sp, m, layer, 0, k, raw[:, k, :], landed[k])
                for t in range(NT):
                    sp.wait_ge(ready, t + 1)
                    sp.dma_start(m.h_dram[t * P:(t + 1) * P, :], h[:, t, :]).then_inc(stored, 16)
                sp.wait_ge(stored, 16 * NT)

            @block.tensor
            def _(pe):
                def turn(t):
                    pe.wait_ge(ready, t + 1)
                    if t >= 1:
                        pe.wait_ge(out, t)
                    for c in range(KC):
                        mm = pe.transpose(ps[:, 4 + c // 4, (c % 4) * P:(c % 4 + 1) * P], h[:, t, c::KC], m.c(C_ID))
                    mm.then_inc(turned, 1)

                def logits(t):
                    pe.wait_ge(out, t + 1)
                    for c in range(KC):
                        pe.matmul(ps[:, 6, t * ROUTES:(t + 1) * ROUTES], hT[:, c, t * P:(t + 1) * P], w_route[:, c, :],
                                  start=(c == 0), stop=(c == KC - 1))

                for t in range(NT):
                    rows = slice(t * P, (t + 1) * P)
                    pe.wait_ge(y_split, t + 1)
                    if t >= 2:
                        pe.wait_ge(summed, t - 1)
                    for c in range(KC):
                        if t == 0:
                            pe.wait_ge(w_split, c + 1)
                        for hf in range(2):
                            cols = slice(hf * HALF, (hf + 1) * HALF)
                            mm = three(pe, ps[:, 2 * (t % 2) + hf, :], (y_hi[:, c, rows], y_lo[:, c, rows]),
                                       (w_hi[:, c, cols], w_lo[:, c, cols]), c == 0, c == KC - 1)
                    mm.then_inc(proj, 1)
                    if t == 1:
                        pe.wait_ge(s_wr, 16)
                    if t:
                        turn(t - 1)
                    if t >= 2:
                        logits(t - 2)
                turn(NT - 1)
                logits(NT - 2)
                logits(NT - 1)

            @block.vector
            def _(v):
                steps = Steps(v, s_dve)
                steps.link(v.memset(norm.eps[:], LN_EPS))
                for kind, n in order:
                    if kind == "y":
                        v.wait_ge(y_taken, n + 1)
                        rows = slice(n * P, (n + 1) * P)
                        take_low(v, y_lo[:, :, rows], hT[:, :, rows], y_hi[:, :, rows]).then_inc(y_split, 1)
                    else:
                        v.wait_ge(w_taken, n + 1)
                        take_low(v, w_lo[:, n, :], w_out[:, n, :], w_hi[:, n, :]).then_inc(w_split, 1)
                v.wait_ge(s_ln, 16)
                for t in range(NT):
                    v.wait_ge(proj, t + 1)
                    x = h[:, t, :].rearrange("p (u f) -> p u f", u=2)
                    v.scalar_tensor_tensor(x, x, ALPHA, ps[:, 2 * (t % 2):2 * (t % 2) + 2, :], ALU.mult, ALU.add
                                           ).then_inc(summed, 1)
                    v.wait_ge(summed, t + 1)
                    norm.statistics(v, steps, t)
                    norm.scale(v, steps, t)
                    norm.gain(v, t)

            @block.scalar
            def _(act):
                for kind, n in order:
                    if kind == "y":
                        rows = slice(n * P, (n + 1) * P)
                        act.activation(y_hi[:, :, rows], hT[:, :, rows], ACT.Copy).then_inc(y_taken, 1)
                    else:
                        act.wait_ge(s_w[n // 2], 16)
                        act.activation(w_hi[:, n, :], w_out[:, n, :], ACT.Copy).then_inc(w_taken, 1)
                for t in range(NT + 1):
                    if t < NT:
                        norm.root(act, t)
                        norm.normalise(act, t)
                    if t:
                        act.wait_ge(turned, t)
                        act.activation(hT[:, :, (t - 1) * P:t * P],
                                       ps[:, 4:6, :].rearrange("p b (c w) -> p (b c) w", w=P), ACT.Copy).then_inc(out, 1)


def load_piece(sp, m, layer, e, k, dst, landed):
    name = ("moe_w_gate", "moe_w_up", "moe_w_down")[k // 2]
    w = m.a[name][layer, bass.ds(e, 1)]
    if k < 4:
        src, steps = w.rearrange("e (p c) f -> p (e c) f", c=KC), KC // 2
    else:
        src, steps = w.rearrange("e (c p) f -> p (e c) f", c=FC), FC // 2
    at = (k % 2) * steps
    sp.dma_start(dst.rearrange("p (c f) -> p c f", c=steps), src[:, at:at + steps, :]).then_inc(landed, 16)


def router(m, layer):
    nc, a, sb, sem, ps, hT, cst = m.nc, m.a, m.sb, m.sem, m.ps, m.hT, m.cst
    scope = ExitStack()
    n_ = lambda x: f"{x}_r{layer}"
    with scope:
        lg = sb(n_("lg"), [P, NT, GROUPS], scope=scope)
        el = sb(n_("el"), [P, NT, EXPERTS], scope=scope)
        cand = sb(n_("cand"), [P, 2, NT, EXPERTS], scope=scope)
        one = sb(n_("one"), [P, 2, NT, EXPERTS], scope=scope)
        both = sb(n_("both"), [P, NT, EXPERTS], scope=scope)
        g4 = sb(n_("g4"), [P, 2, NT, GROUPS], scope=scope)
        k = sb(n_("k"), [P, 20, NT], scope=scope)
        base = sb(n_("base"), [P, NT + 1, EXPERTS], scope=scope)
        ov = sb(n_("ov"), [P, 4, EXPERTS], scope=scope)
        tmp = sb(n_("tmp"), [P, 2, EXPERTS], scope=scope)
        slot = sb(n_("slot"), [P, 2, NT, P], scope=scope)
        blk = sb(n_("blk"), [P, 2, NT, TABLE], scope=scope)
        tab = sb(n_("tab"), [P, 3, TABLE], scope=scope)
        cnt = sb(n_("cnt"), [1, TABLE - EXPERTS, EXPERTS], scope=scope)
        ids = sb(n_("ids"), [1, TABLE + 1], scope=scope)
        s_exp, exp_out, onehots, prefixed, s_dve, assigned, tabled = (sem(n_(x)) for x in
            ("exp_in", "exp_out", "onehots", "prefixed", "dve", "assigned", "tabled"))
        with nc.Block() as block:
            @block.tensor
            def _(pe):
                pe.wait_ge(onehots, 1)
                flat = both[:].rearrange("p t e -> p (t e)")
                pe.matmul(ps[:, 1, 0:NT * EXPERTS], m.c(C_USTRICT), flat, start=True, stop=True)
                pe.matmul(ps[:, 2, 0:NT * EXPERTS], m.c(C_ONES), flat, start=True, stop=True).then_inc(prefixed, 1)
                pe.wait_ge(assigned, 1)
                for x in range(2):
                    for t in range(NT):
                        mm = pe.matmul(ps[:, 3, 0:TABLE], slot[:, x, t, :], blk[:, x, t, :],
                                       start=(x + t == 0), stop=(x == 1 and t == NT - 1))
                mm.then_inc(tabled, 1)

            @block.scalar
            def _(act):
                act.wait_ge(s_exp, 1)
                act.activation(g4[:, 1], g4[:, 1], ACT.Exp).then_inc(exp_out, 1)
                act.wait_ge(s_exp, 2)
                act.activation(k[:, 5, :], k[:, 5, :], ACT.Exp).then_inc(exp_out, 1)

            @block.vector
            def _(v):
                steps = Steps(v, s_dve)
                link = steps.link
                bc = lambda x, n: x[:, :, None].to_broadcast([P, NT, n])
                iota = lambda n: cst[:, None, C_IOTA:C_IOTA + n].to_broadcast([P, NT, n])
                rt = R_ROUTE + layer * ROUTES

                def first_of_largest(index, largest, values, scratch, n):
                    link(v.tensor_reduce(largest, values, AX, ALU.max))
                    link(v.tensor_tensor(scratch, values, bc(largest, n), ALU.is_ge))
                    link(v.scalar_tensor_tensor(scratch, scratch, -100.0, iota(n), ALU.mult, ALU.add))
                    link(v.tensor_reduce(index, scratch, AX, ALU.min))
                    link(v.tensor_scalar(index, index, 100.0, None, ALU.add))

                raw = ps[:, 6, 0:NT * ROUTES].rearrange("p (t r) -> p t r", r=ROUTES)
                link(v.tensor_tensor(lg[:], raw[:, :, 0:GROUPS],
                                     m.rows[:, None, rt:rt + GROUPS].to_broadcast([P, NT, GROUPS]), ALU.add))
                link(v.tensor_tensor(el[:], raw[:, :, GROUPS:],
                                     m.rows[:, None, rt + GROUPS:rt + ROUTES].to_broadcast([P, NT, EXPERTS]), ALU.add))
                first_of_largest(k[:, 1, :], k[:, 0, :], lg[:], g4[:, 0], GROUPS)
                v.tensor_tensor(g4[:, 1], lg[:], bc(k[:, 0, :], GROUPS), ALU.subtract).then_inc(s_exp, 1)
                link(v.tensor_tensor(g4[:, 0], iota(GROUPS), bc(k[:, 1, :], GROUPS), ALU.is_equal))
                link(v.tensor_scalar(g4[:, 0], g4[:, 0], 1.0, 1e30, ALU.subtract, ALU.mult))
                eg = el[:].rearrange("p t (g j) -> p (t g) j", j=PER_GROUP)
                link(v.tensor_tensor(eg, eg, g4[:, 0].rearrange("p t g -> p (t g)")[:, :, None]
                                     .to_broadcast([P, NT * GROUPS, PER_GROUP]), ALU.add))
                for x in range(2):
                    first_of_largest(k[:, 6 + x, :], k[:, 3 + x, :], el[:], cand[:, 0], EXPERTS)
                    link(v.tensor_tensor(one[:, x], iota(EXPERTS), bc(k[:, 6 + x, :], EXPERTS), ALU.is_equal))
                    if x == 0:
                        link(v.scalar_tensor_tensor(el[:], one[:, 0], -2e30, el[:], ALU.mult, ALU.add))
                v.tensor_tensor(both[:], one[:, 0], one[:, 1], ALU.add).then_inc(onehots, 1)
                v.tensor_tensor(k[:, 5, :], k[:, 4, :], k[:, 3, :], ALU.subtract).then_inc(s_exp, 1)
                v.wait_ge(exp_out, 2)
                link(v.tensor_reduce(k[:, 2, :], g4[:, 1], AX, ALU.add))
                link(v.tensor_scalar(k[:, 18, :], k[:, 5, :], 1.0, None, ALU.add))
                link(v.tensor_tensor(k[:, 2, :], k[:, 2, :], k[:, 18, :], ALU.mult))
                link(v.reciprocal(m.gates[:, 0, :], k[:, 2, :]))
                link(v.tensor_tensor(m.gates[:, 1, :], m.gates[:, 0, :], k[:, 5, :], ALU.mult))
                v.wait_ge(prefixed, 1)
                within = ps[:, 1, 0:NT * EXPERTS].rearrange("p (t e) -> p t e", e=EXPERTS)
                totals = ps[:, 2, 0:NT * EXPERTS].rearrange("p (t e) -> p t e", e=EXPERTS)
                v.memset(base[:, 0, :], 0.0)
                link(v.memset(tmp[:, 0, :], 1.0))
                for t in range(NT):
                    link(v.tensor_tensor(base[:, t + 1, :], base[:, t, :], totals[:, t, :], ALU.add))
                link(v.tensor_tensor(both[:], base[:, 0:NT, :], within, ALU.add))
                magic, down = float(1.5 * 2 ** 23), 127.0 / 256.0
                count = base[:, NT, :]
                link(v.tensor_scalar(ov[:, 0, :], count, 1.0 / P, -1.0 / P - down, ALU.mult, ALU.add))
                link(v.tensor_scalar(ov[:, 0, :], ov[:, 0, :], magic, None, ALU.add))
                link(v.tensor_scalar(ov[:, 0, :], ov[:, 0, :], magic, 0.0, ALU.subtract, ALU.max))
                link(v.tensor_tensor_scan(ov[:, 1, :], tmp[:, 0, :], ov[:, 0, :], 0.0, ALU.mult, ALU.add))
                link(v.tensor_tensor(ov[:, 2, :], ov[:, 1, :], ov[:, 0, :], ALU.subtract))
                NK = 2 * NT
                e, rank, first, hi, bl, used = (k[:, a:a + 2, :].rearrange("p x t -> p (x t)") for a in (6, 8, 10, 12, 14, 16))
                picked = one[:].rearrange("p x t e -> p (x t) e")
                wide = lambda x, n: x[:, :, None].to_broadcast([P, NK, n])
                for x in range(2):
                    link(v.tensor_tensor(cand[:, x], one[:, x], both[:], ALU.mult))
                link(v.tensor_tensor(picked, picked, ov[:, 2:3, :].to_broadcast([P, NK, EXPERTS]), ALU.mult))
                v.tensor_reduce(rank, cand[:].rearrange("p x t e -> p (x t) e"), AX, ALU.add)
                link(v.tensor_reduce(first, picked, AX, ALU.add))
                link(v.tensor_scalar(hi, rank, 1.0 / P, -down, ALU.mult, ALU.add))
                link(v.tensor_scalar(hi, hi, magic, None, ALU.add))
                link(v.tensor_scalar(hi, hi, magic, None, ALU.subtract))
                link(v.tensor_tensor(bl, first, hi, ALU.add))
                v.tensor_scalar(used, hi, 1.0, None, ALU.min)
                link(v.scalar_tensor_tensor(bl, bl, float(EXPERTS - 1), e, ALU.add, ALU.subtract))
                link(v.tensor_tensor(bl, bl, used, ALU.mult))
                v.scalar_tensor_tensor(rank, hi, -float(P), rank, ALU.mult, ALU.add)
                link(v.tensor_tensor(bl, bl, e, ALU.add))
                iota_of = lambda n: cst[:, None, C_IOTA:C_IOTA + n].to_broadcast([P, NK, n])
                v.tensor_tensor(slot[:].rearrange("p x t w -> p (x t) w"), iota_of(P), wide(rank, P), ALU.is_equal)
                blocks = blk[:].rearrange("p x t w -> p (x t) w")
                link(v.tensor_tensor(blocks, iota_of(TABLE), wide(bl, TABLE), ALU.is_equal))
                v.tensor_tensor(blocks, blocks, cst[:, C_TOKEN:C_TOKEN + NK, None].to_broadcast([P, NK, TABLE]), ALU.mult
                                ).then_inc(assigned, 1)
                inc = ov[0:1, 1, :]
                nb = TABLE - EXPERTS
                link(v.tensor_tensor(cnt[:], inc[:, None, :].to_broadcast([1, nb, EXPERTS]),
                                     cst[0:1, C_IOTA:C_IOTA + nb, None].to_broadcast([1, nb, EXPERTS]), ALU.is_le))
                link(v.tensor_reduce(ids[:, EXPERTS:TABLE], cnt[:], AX, ALU.add))
                link(v.tensor_scalar(ids[:, EXPERTS:TABLE], ids[:, EXPERTS:TABLE], float(EXPERTS - 1), None, ALU.min))
                link(v.tensor_copy(ids[:, 0:EXPERTS], cst[0:1, C_IOTA:C_IOTA + EXPERTS]))
                link(v.tensor_scalar(tmp[0:1, 0, 0:8], cst[0:1, C_STEP:C_STEP + 8], inc[:, EXPERTS - 1:EXPERTS], None, ALU.is_lt))
                link(v.tensor_reduce(ids[:, TABLE:], tmp[0:1, 0, 0:8], AX, ALU.add))
                link(v.tensor_scalar(ids[:, TABLE:], ids[:, TABLE:], float(EXPERTS // 2), None, ALU.add))
                link(v.tensor_copy(m.ctl[:], ids[:]))
                v.wait_ge(tabled, 1)
                val, none, row = tab[:, 0, :], tab[:, 1, :], tab[:, 2, :]
                link(v.tensor_copy(val, ps[:, 3, 0:TABLE]))
                link(v.tensor_scalar(none, val, 0.0, float(NOBODY), ALU.is_equal, ALU.mult))
                link(v.scalar_tensor_tensor(row, val, -1.0, none, ALU.add, ALU.add))
                link(v.tensor_copy(m.dst_idx[:], row))
                link(v.tensor_scalar(val, val, float(SEQ), -float(SEQ), ALU.is_gt, ALU.mult))
                link(v.tensor_tensor(row, row, val, ALU.add))
                link(v.tensor_copy(m.src_idx[:], row))


def expert_blocks(m, layer, raw, landed):
    nc, a, sb, sem, ps, cst, hT = m.nc, m.a, m.sb, m.sem, m.ps, m.cst, m.hT
    scope = ExitStack()
    n_ = lambda x: f"{x}_e{layer}"
    with scope:
        w_hi = sb(n_("w_hi"), [P, PIECES, PIECE], F32R, scope=scope)
        w_lo = sb(n_("w_lo"), [P, PIECES, PIECE], F32R, scope=scope)
        x_hi = sb(n_("x_hi"), [P, KC, P], F32R, scope=scope)
        x_lo = sb(n_("x_lo"), [P, KC, P], F32R, scope=scope)
        hid_hi = sb(n_("hid_hi"), [P, FC, P], F32R, scope=scope)
        hid_lo = sb(n_("hid_lo"), [P, FC, P], F32R, scope=scope)
        idx = sb(n_("idx"), [P, 2, 2], I32, scope=scope)
        x, y = hT[:, 0:2, :], hT[:, 2:4, :]
        act_g, hid = hT[:, 4, 0:F], hT[:, 4, F:2 * F]
        ring = [raw[:, slot, :] for slot in range(RING - 1)] + [hT[:, 6:8, :].rearrange("p a b -> p (a b)")]

        taken, split, used = sem(n_("taken")), sem(n_("split")), sem(n_("used"))
        x_turned, x_high, x_split, silu, upped, hid_out, h_turned, h_high, h_split, y_out, y_free = (sem(n_(q)) for q in
            ("x_turned", "x_high", "x_split", "silu", "upped", "hid_out", "h_turned", "h_high", "h_split", "y_out", "y_free"))
        idx_src, idx_dst, go = sem(n_("idx_src")), sem(n_("idx_dst")), sem(n_("dma_may_go"))
        gathered = [sem(n_(f"gathered{j}")) for j in range(2)]
        scattered = [sem(n_(f"scattered{j}")) for j in range(2)]

        def every_block(eng, body):
            for j in range(2):
                body(0, j)
            n = eng.value_load(m.ctl[0:1, TABLE:TABLE + 1], min_val=EXPERTS // 2, max_val=BLOCKS // 2)
            with eng.Fori(0, n - 1) as i:
                for j in range(2):
                    body(i + 1, j)
            return n

        peeled = lambda q: isinstance(q, int)

        with nc.Block() as block:
            @block.sync
            def _(sp):
                def loads(q, j):
                    b = 2 * q + j
                    e = b if peeled(q) else sp.value_load(m.ctl[0:1, bass.ds(b, 1)], min_val=0, max_val=EXPERTS - 1)
                    for k in range(PIECES):
                        if peeled(q) and b == 0 and k < RING - 1:
                            continue
                        slot = (PIECES * j + k) % RING
                        if not (peeled(q) and b == 0 and k < RING):
                            sp.wait_ge(split, PIECES * b + k - RING + 1)
                        load_piece(sp, m, layer, e, k, ring[slot], landed[slot])

                every_block(sp, loads)

            @block.gpsimd
            def _(pool):
                last_token, last_row = pool.to_reg(SEQ - 1), pool.to_reg(2 * SEQ - 1)

                def gather(b, j, before):
                    if before is not None:
                        pool.wait_ge(gathered[j], 16 * before)
                    pool.tensor_copy(idx[:, j, 0:1], m.src_idx[:, bass.ds(b, 1)]).then_inc(idx_src, 1)
                    pool.wait_ge(idx_src, b + 1)
                    if before is not None:
                        pool.wait_ge(x_turned, b - 1)
                    pool.sem_inc(go, 1)
                    pool.indirect_dma_start(x[:, j, :], None, m.h_dram, bass.IndirectOffsetOnAxis(ap=idx[:, j, 0:1], axis=0),
                                            bounds_check=last_token, oob_is_err=False).then_inc(gathered[j], 16)

                def body(q, j):
                    b = 2 * q + j
                    first = peeled(q) and b == 0
                    gather(b + 1, 1 - j, None if first else q + j)
                    if not peeled(q):
                        pool.wait_ge(scattered[j], 16 * q)
                    pool.sem_inc(y_free, 1)
                    pool.tensor_copy(idx[:, j, 1:2], m.dst_idx[:, bass.ds(b, 1)]).then_inc(idx_dst, 1)
                    pool.wait_ge(idx_dst, b + 1)
                    pool.wait_ge(y_out, b + 1)
                    pool.sem_inc(go, 1)
                    pool.indirect_dma_start(m.y_dram, bass.IndirectOffsetOnAxis(ap=idx[:, j, 1:2], axis=0), y[:, j, :], None,
                                            bounds_check=last_row, oob_is_err=False).then_inc(scattered[j], 16)

                gather(0, 0, None)
                n = every_block(pool, body)
                for j in range(2):
                    pool.wait_ge(scattered[j], 16 * n)
                pool.wait_ge(gathered[0], 16 * n + 16)
                pool.wait_ge(gathered[1], 16 * n)

            @block.tensor
            def _(pe):
                def turn_x(j, k):
                    pe.wait_ge(gathered[j], 16 * k)
                    for c in range(KC):
                        mm = pe.transpose(ps[:, c // 4, (c % 4) * P:(c % 4 + 1) * P], x[:, j, c::KC], m.c(C_ID))
                    mm.then_inc(x_turned, 1)

                def weights(piece, cols):
                    return w_hi[:, piece, cols], w_lo[:, piece, cols]

                def body(q, j):
                    b = 2 * q + j
                    pe.wait_ge(x_split, b + 1)
                    for c in range(KC):
                        k = c // 4
                        if c % 4 == 0:
                            pe.wait_ge(split, PIECES * b + k + 1)
                        mm = three(pe, ps[:, 2, :], (x_hi[:, c, :], x_lo[:, c, :]),
                                   weights(k, slice((c % 4) * F, (c % 4 + 1) * F)), c == 0, c == KC - 1)
                        if c % 4 == 3:
                            mm.then_inc(used, 1)
                    for half in range(2):
                        for c in range(KC):
                            k = 2 + c // 4
                            if c % 4 == 0 and half == 0:
                                pe.wait_ge(split, PIECES * b + k + 1)
                            at = (c % 4) * F + half * (F // 2)
                            mm = three(pe, ps[:, 3 + half, 0:F // 2], (x_hi[:, c, :], x_lo[:, c, :]),
                                       weights(k, slice(at, at + F // 2)), c == 0, c == KC - 1)
                            if half and c % 4 == 3:
                                mm.then_inc(used, 1)
                        if half == 0:
                            mm.then_inc(upped, 1)
                    turn_x(1 - j, q + j + 1)
                    for half in range(2):
                        pe.wait_ge(hid_out, 2 * b + half + 1)
                        for c in range(2 * half, 2 * half + 2):
                            mm = pe.transpose(ps[:, 5 - 3 * half, c * P:(c + 1) * P], hid[:, c * P:(c + 1) * P], m.c(C_ID))
                        mm.then_inc(h_turned, 1)
                    pe.wait_ge(h_split, 2 * b + 2)
                    if not (peeled(q) and b == 0):
                        pe.wait_ge(y_out, b)
                    for half in range(2):
                        for c in range(FC):
                            k = 4 + c // 2
                            if c % 2 == 0 and half == 0:
                                pe.wait_ge(split, PIECES * b + k + 1)
                            at = (c % 2) * D + half * HALF
                            mm = three(pe, ps[:, 6 + half, :], (hid_hi[:, c, :], hid_lo[:, c, :]),
                                       weights(k, slice(at, at + HALF)), c == 0, c == FC - 1)
                            if half and c % 2 == 1:
                                mm.then_inc(used, 1)

                turn_x(0, 1)
                every_block(pe, body)

            @block.scalar
            def _(act):
                def take(q, j, k):
                    b, nth = 2 * q + j, PIECES * j + k
                    act.wait_ge(landed[nth % RING], 16 * (2 * PIECES // RING * q + nth // RING + 1))
                    if not (peeled(q) and b == 0):
                        act.wait_ge(used, PIECES * (b - 1) + k + 1)
                    act.activation(w_hi[:, k, :], ring[nth % RING], ACT.Copy).then_inc(taken, 1)

                def take_x(b):
                    act.wait_ge(x_turned, b + 1)
                    act.activation(x_hi[:].rearrange("p c w -> p (c w)"), ps[:, 0:2, :].rearrange("p b f -> p (b f)"),
                                   ACT.Copy).then_inc(x_high, 1)

                def copy_y(b, j):
                    act.wait_ge(used, PIECES * b + PIECES)
                    act.wait_ge(y_free, b + 1)
                    act.activation(y[:, j, :], ps[:, 6:8, :].rearrange("p b f -> p (b f)"), ACT.Copy).then_inc(y_out, 1)

                def body(q, j):
                    b = 2 * q + j
                    take(q, j, 0)
                    take_x(b)
                    for k in range(1, 4):
                        take(q, j, k)
                    if not (peeled(q) and b == 0):
                        copy_y(b - 1, 1 - j)
                    act.wait_ge(used, PIECES * b + 2)
                    act.activation(act_g, ps[:, 2, :], ACT.Silu).then_inc(silu, 1)
                    take(q, j, 4)
                    take(q, j, 5)
                    for half in range(2):
                        act.wait_ge(h_turned, 2 * b + half + 1)
                        act.activation(hid_hi[:, 2 * half:2 * half + 2, :].rearrange("p c w -> p (c w)"),
                                       ps[:, 5 - 3 * half, half * 2 * P:(half + 1) * 2 * P], ACT.Copy).then_inc(h_high, 1)

                n = every_block(act, body)
                copy_y(2 * n - 1, 1)

            @block.vector
            def _(v):
                def rest(q, j, k):
                    v.wait_ge(taken, PIECES * (2 * q + j) + k + 1)
                    v.tensor_tensor(w_lo[:, k, :], ring[(PIECES * j + k) % RING], w_hi[:, k, :].bitcast(F32), ALU.subtract
                                    ).then_inc(split, 1)

                def rest_x(b):
                    v.wait_ge(x_high, b + 1)
                    v.tensor_tensor(x_lo[:].rearrange("p c w -> p (c w)"), ps[:, 0:2, :].rearrange("p b f -> p (b f)"),
                                    x_hi[:].bitcast(F32).rearrange("p c w -> p (c w)"), ALU.subtract).then_inc(x_split, 1)

                def body(q, j):
                    b = 2 * q + j
                    rest(q, j, 0)
                    rest_x(b)
                    for k in range(1, 5):
                        rest(q, j, k)
                    v.wait_ge(silu, b + 1)
                    v.wait_ge(upped, b + 1)
                    v.tensor_tensor(hid[:, 0:F // 2], act_g[:, 0:F // 2], ps[:, 3, 0:F // 2], ALU.mult).then_inc(hid_out, 1)
                    v.wait_ge(used, PIECES * b + 4)
                    v.tensor_tensor(hid[:, F // 2:], act_g[:, F // 2:], ps[:, 4, 0:F // 2], ALU.mult).then_inc(hid_out, 1)
                    rest(q, j, 5)
                    for half in range(2):
                        v.wait_ge(h_high, 2 * b + half + 1)
                        v.tensor_tensor(hid_lo[:, 2 * half:2 * half + 2, :].rearrange("p c w -> p (c w)"),
                                        ps[:, 5 - 3 * half, half * 2 * P:(half + 1) * 2 * P],
                                        hid_hi[:, 2 * half:2 * half + 2, :].bitcast(F32).rearrange("p c w -> p (c w)"),
                                        ALU.subtract).then_inc(h_split, 1)

                every_block(v, body)


def combine(m, layer, out):
    nc, a, sb, sem, ps, h, hT = m.nc, m.a, m.sb, m.sem, m.ps, m.h, m.hT
    scope = ExitStack()
    n_ = lambda x: f"{x}_c{layer}"
    with scope:
        ln = sb(n_("ln"), [P, 2, D], scope=scope)
        y = sb(n_("y"), [P, 4, 2, D], scope=scope)
        norm = LayerNorm(m, n_("norm"), scope, ln[:, 0, :], ln[:, 1, :])
        ready = norm.ready
        s_y = [sem(n_(f"y_in{q}")) for q in range(4)]
        s_ln, weighted, summed, turned, copied, stored, s_dve = (sem(n_(x)) for x in
            ("ln_in", "weighted", "summed", "turned", "ht_out", "stored", "dve"))
        with nc.Block() as block:
            @block.gpsimd
            def _(pool):
                pool.wait_ge(s_ln, 16)
                for t in range(NT):
                    norm.gain(pool, t)
                    norm.shift(pool, t)

            @block.sync
            def _(sp):
                sp.dma_start(ln[:], a["ln"][layer, 1].partition_broadcast(P)).then_inc(s_ln, 16)
                rows = m.y_dram.rearrange("(k t p) d -> t p k d", k=2, p=P)
                for t in range(NT):
                    if t >= 4:
                        sp.wait_ge(summed, t - 3)
                    sp.dma_start(y[:, t % 4], rows[t]).then_inc(s_y[t % 4], 16)
                    if out is not None and t >= 3:
                        sp.wait_ge(ready, t - 2)
                        sp.dma_start(out[0, (t - 3) * P:(t - 2) * P, :], h[:, t - 3, :]).then_inc(stored, 16)
                if out is not None:
                    for t in range(NT - 3, NT):
                        sp.wait_ge(ready, t + 1)
                        sp.dma_start(out[0, t * P:(t + 1) * P, :], h[:, t, :]).then_inc(stored, 16)
                    sp.wait_ge(stored, 16 * NT)

            @block.vector
            def _(v):
                steps = Steps(v, s_dve)
                steps.link(v.memset(norm.eps[:], LN_EPS))
                v.wait_ge(s_ln, 16)
                for t in range(NT):
                    x = h[:, t, :]
                    v.wait_ge(weighted, t + 1)
                    v.wait_ge(s_y[t % 4], 16 * (t // 4 + 1))
                    steps.link(v.scalar_tensor_tensor(x, y[:, t % 4, 0, :], m.gates[:, 0, t:t + 1], x, ALU.mult, ALU.add))
                    v.scalar_tensor_tensor(x, y[:, t % 4, 1, :], m.gates[:, 1, t:t + 1], x, ALU.mult, ALU.add
                                           ).then_inc(summed, 1)
                    v.wait_ge(summed, t + 1)
                    norm.statistics(v, steps, t)
                    norm.scale(v, steps, t)

            @block.tensor
            def _(pe):
                for t in range(NT if out is None else 0):
                    pe.wait_ge(ready, t + 1)
                    if t >= 2:
                        pe.wait_ge(copied, t - 1)
                    for c in range(KC):
                        mm = pe.transpose(ps[:, 2 * (t % 2) + c // 4, (c % 4) * P:(c % 4 + 1) * P], h[:, t, c::KC], m.c(C_ID))
                    mm.then_inc(turned, 1)

            @block.scalar
            def _(act):
                for t in range(NT):
                    act.activation(h[:, t, :], h[:, t, :], ACT.Copy, scale=ALPHA).then_inc(weighted, 1)
                for t in range(NT + 1):
                    if t < NT:
                        norm.root(act, t)
                        norm.normalise(act, t)
                    if t and out is None:
                        act.wait_ge(turned, t)
                        act.activation(hT[:, :, (t - 1) * P:t * P],
                                       ps[:, 2 * ((t - 1) % 2):2 * ((t - 1) % 2) + 2, :].rearrange("p b (c w) -> p (b c) w", w=P),
                                       ACT.Copy).then_inc(copied, 1)


def lay_out(x, positions, hyb_w_in, hyb_sinks, hyb_conv_w, hyb_a_log, hyb_dt_bias, hyb_norm_g,
            hyb_w_out, rec_w_in, rec_conv_w, rec_conv_b, rec_w_a, rec_b_a, rec_w_x, rec_b_x,
            rec_lambda, rec_w_out, moe_rg_w, moe_rg_b, moe_re_w, moe_re_b, moe_w_gate, moe_w_up,
            moe_w_down, ln_g, ln_b):
    def by_row(w):
        return w.reshape(P, KC, w.shape[-1])

    def tiles(w):
        return by_row(w).reshape(P, KC, -1, P).transpose(2, 0, 1, 3)

    w = hyb_w_in[0]
    q = w[:, 0:512].reshape(D, 2, 4, A_HD).transpose(0, 2, 1, 3).reshape(D, 512)
    ch = np.concatenate([q, w[:, 512:640], w[:, 768:2304]], axis=1)
    cols = lambda v: v.reshape(KC, P).T
    rec = rec_w_in[0]
    out = {
        "x": x[0],
        "xT": by_row(x[0].T),
        "positions": positions[0],
        "cst": constants(),
        "rows": np.concatenate([hyb_sinks[0], hyb_a_log[0], hyb_dt_bias[0], hyb_norm_g[0],
                                moe_rg_b[0], moe_re_b[0], moe_rg_b[1], moe_re_b[1]]),
        "w_ch": tiles(ch),
        "w_vs": by_row(np.concatenate([w[:, 640:768], w[:, 2816:2824]], axis=1)),
        "w_z": by_row(w[:, 2304:2816]),
        "conv_w": hyb_conv_w[0].T.reshape(12, P, CONV).transpose(1, 0, 2),
        "w_out": np.stack([hyb_w_out[0], rec_w_out[0]]).reshape(2, KC, P, D).transpose(0, 2, 1, 3),
        "rec_w_ch": tiles(np.concatenate([rec[:, D:], rec[:, :D]], axis=1)),
        "rec_vec": np.stack([cols(v) for v in (*rec_conv_w[0], rec_conv_b[0], rec_b_a[0], rec_b_x[0], rec_lambda[0])], axis=1),
        "w_ax": np.stack([rec_w_a[0], rec_w_x[0]]).reshape(2, 4, 2, P, 2 * P).transpose(3, 0, 1, 2, 4),
        "w_route": np.concatenate([moe_rg_w, moe_re_w], axis=2).reshape(2, P, KC, ROUTES),
        "moe_w_gate": moe_w_gate,
        "moe_w_up": moe_w_up,
        "moe_w_down": moe_w_down,
        "ln": np.stack([ln_g, ln_b], axis=2),
    }
    return {k: np.ascontiguousarray(v) for k, v in out.items()}


def kernel(**inputs):
    from concourse import bacc
    from concourse.bass_utils import run_bass_kernel_spmd

    arrays = lay_out(**{k: np.asarray(v) for k, v in inputs.items()})
    nc = bacc.Bacc("TRN2", target_bir_lowering=False, num_devices=1)
    a = {k: nc.dram_tensor(f"in_{k}", v.shape, mybir.dt.from_np(v.dtype), kind="ExternalInput").ap() for k, v in arrays.items()}
    out = nc.dram_tensor("out", (1, SEQ, D), F32, kind="ExternalOutput").ap()
    program(nc, a, out)
    r = run_bass_kernel_spmd(nc, [{f"in_{k}": v for k, v in arrays.items()}], core_ids=[0])
    return r.results[0]["out"]
```
